# Optimizing a Trainium2 kernel written in Bass

```python
import jax, jax.numpy as jnp
from jax import lax
import numpy as np

D_MODEL = 1024
BATCH = 1
SEQ = 256
DEPTH = 2
DEC_BATCH = 1
DEC_SEQ = 32
PAST_LEN = 512

CHUNK = 64
PLE_DIM = 256
MLA_HEADS = 8
NOPE_DIM = 64
ROPE_DIM = 32
V_DIM = 64
Q_LORA = 384
KV_LORA = 256
ROPE_THETA = 10000.0
Q_BLOCK = 128
ATTN_SCALE = (NOPE_DIM + ROPE_DIM) ** -0.5
HG_HEADS = 4
HG_DK = 128
HG_DV = 128
HG_FDIM = HG_HEADS * HG_DK
HG_IDIM = HG_HEADS * HG_DV
HG_BLOCK = 16
N_GROUPS = 4
EXPERTS_PER_GROUP = 8
N_EXPERTS = N_GROUPS * EXPERTS_PER_GROUP
TOP_K = 2
D_EXPERT = 512
MOE_BLOCK = 128
DN_ALPHA = (2 * DEPTH) ** 0.25
DN_BETA = (8 * DEPTH) ** -0.25
EPS = 1e-6
SPLITS = (Q_LORA, KV_LORA, ROPE_DIM, HG_FDIM, HG_FDIM, HG_IDIM, HG_IDIM, D_MODEL, D_MODEL)
D_IN = Q_LORA + KV_LORA + ROPE_DIM + 2 * HG_FDIM + 2 * HG_IDIM + 2 * D_MODEL

kernel_name = 'hybrid_mla_hgrn2_hmoe_stream_step'

def layernorm(x, g, b):
    xf = x.astype(jnp.float32)
    mu = xf.mean(-1, keepdims=True)
    var = jnp.square(xf - mu).mean(-1, keepdims=True)
    return ((xf - mu) * lax.rsqrt(var + EPS)).astype(x.dtype) * g + b

def rmsnorm(x, g):
    xf = x.astype(jnp.float32)
    return (xf * lax.rsqrt(jnp.square(xf).mean(-1, keepdims=True) + EPS)).astype(x.dtype) * g

def rope(x, pos):
    half = ROPE_DIM // 2
    inv = ROPE_THETA ** (-jnp.arange(half, dtype=jnp.float32) / half)
    ang = pos.astype(jnp.float32)[:, None] * inv[None, :]
    shape = (1, x.shape[1]) + (1,) * (x.ndim - 3) + (half,)
    c, s = jnp.cos(ang).reshape(shape), jnp.sin(ang).reshape(shape)
    xf = x.astype(jnp.float32)
    x1, x2 = xf[..., :half], xf[..., half:]
    return jnp.concatenate([x1 * c - x2 * s, x2 * c + x1 * s], axis=-1).astype(x.dtype)

def mla_prompt_attention(q_nope, q_rope, ckv, k_rope, w_uk, w_uv):
    B, S = ckv.shape[:2]
    k_nope = jnp.einsum('bsc,chn->bshn', ckv, w_uk)
    v = jnp.einsum('bsc,chv->bshv', ckv, w_uv)
    nqb = S // Q_BLOCK
    key_chunk = jnp.arange(S) // CHUNK

    def block(args):
        qn, qr, j = args
        s = jnp.einsum('bqhn,bkhn->bhqk', qn, k_nope) + jnp.einsum('bqhr,bkr->bhqk', qr, k_rope)
        s = s.astype(jnp.float32) * ATTN_SCALE
        q_chunk = (j * Q_BLOCK + jnp.arange(Q_BLOCK)) // CHUNK
        mask = key_chunk[None, :] <= q_chunk[:, None]
        p = jax.nn.softmax(jnp.where(mask, s, -jnp.inf), axis=-1).astype(v.dtype)
        return jnp.einsum('bhqk,bkhv->bqhv', p, v)

    qn_b = q_nope.reshape(B, nqb, Q_BLOCK, MLA_HEADS, NOPE_DIM).swapaxes(0, 1)
    qr_b = q_rope.reshape(B, nqb, Q_BLOCK, MLA_HEADS, ROPE_DIM).swapaxes(0, 1)
    out = lax.map(block, (qn_b, qr_b, jnp.arange(nqb)))
    return out.swapaxes(0, 1).reshape(B, S, MLA_HEADS * V_DIM)

def mla_sample_attention(q_nope, q_rope, ckv_all, krope_all, w_uk, w_uv):
    B, L = q_nope.shape[:2]
    q_lat = jnp.einsum('bqhn,chn->bqhc', q_nope, w_uk)
    s = jnp.einsum('bqhc,bkc->bhqk', q_lat, ckv_all) + jnp.einsum('bqhr,bkr->bhqk', q_rope, krope_all)
    p = jax.nn.softmax(s.astype(jnp.float32) * ATTN_SCALE, axis=-1).astype(ckv_all.dtype)
    lat = jnp.einsum('bhqk,bkc->bqhc', p, ckv_all)
    out = jnp.einsum('bqhc,chv->bqhv', lat, w_uv)
    return out.reshape(B, L, MLA_HEADS * V_DIM)

def hgrn2_lower_bounds(hg_lb):
    c = jnp.cumsum(jax.nn.softmax(hg_lb.astype(jnp.float32), axis=0), axis=0)
    return c - c[0:1]

def hgrn2_features(f_pre, q_pre, i_pre, lb):
    B, L, _ = f_pre.shape
    z = f_pre.astype(jnp.float32).reshape(B, L, HG_HEADS, HG_DK)
    lb = lb.reshape(HG_HEADS, HG_DK)
    log_f = jnp.logaddexp(jnp.log(lb), jnp.log1p(-lb) + jax.nn.log_sigmoid(z))
    k = (1.0 - lb) * jax.nn.sigmoid(-z)
    q = jax.nn.silu(q_pre.astype(jnp.float32)).reshape(B, L, HG_HEADS, HG_DK)
    v = i_pre.astype(jnp.float32).reshape(B, L, HG_HEADS, HG_DV)
    return q, k, v, log_f

def hgrn2_block(q, k, v, log_f, S0):
    L = q.shape[1]
    b = jnp.cumsum(log_f, axis=1)
    inter = jnp.einsum('blhk,bhkv->blhv', q * jnp.exp(b), S0)
    diff = b[:, :, None] - b[:, None, :]
    causal = (jnp.arange(L)[:, None] >= jnp.arange(L)[None, :])[None, :, :, None, None]
    decay = jnp.exp(jnp.where(causal, diff, -jnp.inf))
    A = jnp.einsum('bthk,btshk,bshk->bhts', q, decay, k)
    o = inter + jnp.einsum('bhts,bshv->bthv', A, v)
    b_end = b[:, -1]
    S = jnp.exp(b_end)[..., None] * S0 + jnp.einsum('bshk,bshv->bhkv', k * jnp.exp(b_end[:, None] - b), v)
    return o, S

def hgrn2_prompt(q, k, v, log_f):
    B, L = q.shape[:2]
    nb = L // HG_BLOCK

    def to_blocks(t):
        return t.reshape((B, nb, HG_BLOCK) + t.shape[2:]).swapaxes(0, 1)

    def step(S, blk):
        qb, kb, vb, fb = blk
        o, S = hgrn2_block(qb, kb, vb, fb, S)
        return S, o

    S0 = jnp.zeros((B, HG_HEADS, HG_DK, HG_DV), jnp.float32)
    S, o = lax.scan(step, S0, (to_blocks(q), to_blocks(k), to_blocks(v), to_blocks(log_f)))
    return o.swapaxes(0, 1).reshape(B, L, HG_HEADS, HG_DV), S

def moe_dispatch(xt, eidx, wts, w1, w3, w2):
    T, D = xt.shape
    A = T * TOP_K
    flat_e = eidx.reshape(A).astype(jnp.int32)
    flat_tok = jnp.repeat(jnp.arange(T, dtype=jnp.int32), TOP_K)
    flat_w = wts.reshape(A)
    order = jnp.argsort(flat_e)
    se, stok, sw = flat_e[order], flat_tok[order], flat_w[order]
    counts = jnp.zeros((N_EXPERTS,), jnp.int32).at[flat_e].add(1)
    start = jnp.cumsum(counts) - counts
    padded = (counts + MOE_BLOCK - 1) // MOE_BLOCK * MOE_BLOCK
    pend = jnp.cumsum(padded)
    pstart = pend - padded
    pos = pstart[se] + jnp.arange(A, dtype=jnp.int32) - start[se]
    n_blk = (A + N_EXPERTS * (MOE_BLOCK - 1) + MOE_BLOCK - 1) // MOE_BLOCK
    buf = jnp.zeros((n_blk * MOE_BLOCK, D), xt.dtype).at[pos].set(xt[stok])
    blk_e = jnp.searchsorted(pend, jnp.arange(n_blk, dtype=jnp.int32) * MOE_BLOCK, side='right')
    blk_e = jnp.minimum(blk_e, N_EXPERTS - 1)

    def expert_block(args):
        xb, e = args
        h = jax.nn.silu(xb @ w1[e]) * (xb @ w3[e])
        return h @ w2[e]

    out = lax.map(expert_block, (buf.reshape(n_blk, MOE_BLOCK, D), blk_e)).reshape(n_blk * MOE_BLOCK, D)
    return jnp.zeros((T, D), xt.dtype).at[stok].add(out[pos] * sw[:, None].astype(xt.dtype))

def hier_moe(x, w_rg, w_re, w1, w3, w2):
    B, L, D = x.shape
    xt = x.reshape(B * L, D)
    T = B * L
    g_prob = jax.nn.softmax((xt @ w_rg).astype(jnp.float32), axis=-1)
    g_top, g_idx = lax.top_k(g_prob, 1)
    e_logits = (xt @ w_re).astype(jnp.float32).reshape(T, N_GROUPS, EXPERTS_PER_GROUP)
    e_logits = jnp.take_along_axis(e_logits, g_idx[:, :, None], axis=1)[:, 0]
    e_top, e_idx = lax.top_k(jax.nn.softmax(e_logits, axis=-1), TOP_K)
    e_top = e_top / e_top.sum(-1, keepdims=True)
    wts = g_top * e_top
    eidx = g_idx * EXPERTS_PER_GROUP + e_idx
    return moe_dispatch(xt, eidx, wts, w1, w3, w2).reshape(B, L, D)

def trunk_layer(x, ple, pos, lp, lb, cache):
    B, L, _ = x.shape
    proj = x @ lp['w_in']
    cq, ckv, kr, f_pre, q_pre, i_pre, g_pre, ga, gb = jnp.split(proj, np.cumsum(SPLITS)[:-1].tolist(), axis=-1)
    q = (rmsnorm(cq, lp['q_norm']) @ lp['w_uq']).reshape(B, L, MLA_HEADS, NOPE_DIM + ROPE_DIM)
    q_nope, q_rope = q[..., :NOPE_DIM], rope(q[..., NOPE_DIM:], pos)
    ckv = rmsnorm(ckv, lp['kv_norm'])
    kr = rope(kr, pos)
    hq, hk, hv, hlogf = hgrn2_features(f_pre, q_pre, i_pre, lb)
    if cache is None:
        a = mla_prompt_attention(q_nope, q_rope, ckv, kr, lp['w_uk'], lp['w_uv'])
        o, S = hgrn2_prompt(hq, hk, hv, hlogf)
    else:
        ckv_all = jnp.concatenate([cache[0], ckv], axis=1)
        kr_all = jnp.concatenate([cache[1], kr], axis=1)
        a = mla_sample_attention(q_nope, q_rope, ckv_all, kr_all, lp['w_uk'], lp['w_uv'])
        o, S = hgrn2_block(hq, hk, hv, hlogf, cache[2].astype(jnp.float32))
    o = o * lax.rsqrt(jnp.square(o).mean(-1, keepdims=True) + EPS) * lp['hg_norm'].reshape(HG_HEADS, HG_DV).astype(jnp.float32)
    o = o * jax.nn.silu(g_pre.astype(jnp.float32)).reshape(B, L, HG_HEADS, HG_DV)
    o = o.reshape(B, L, HG_IDIM).astype(x.dtype)
    merged = jax.nn.sigmoid(ga) * (a @ lp['w_br_a']) + jax.nn.sigmoid(gb) * (o @ lp['w_br_b'])
    x = layernorm(DN_ALPHA * x + merged @ lp['w_out'], lp['ln1_g'], lp['ln1_b'])
    moe_out = hier_moe(x, lp['w_rg'], lp['w_re'], lp['w1'], lp['w3'], lp['w2'])
    ple_term = jax.nn.sigmoid(x @ lp['w_ple_gate']) * (ple @ lp['w_ple'])
    x = layernorm(DN_ALPHA * x + moe_out + ple_term, lp['ln2_g'], lp['ln2_b'])
    return x, ckv, kr, S.astype(x.dtype)

def setup_inputs(seed: int = 0) -> dict:
    key = jax.random.key(seed)
    ks = jax.random.split(key, 40)

    def nrm(k, shape, scale):
        return jax.random.normal(k, shape, jnp.float32) * scale

    col_scale = jnp.concatenate([
        jnp.ones((Q_LORA + KV_LORA + ROPE_DIM + 2 * HG_FDIM,), jnp.float32),
        jnp.full((HG_IDIM,), DN_BETA, jnp.float32),
        jnp.ones((HG_IDIM + 2 * D_MODEL,), jnp.float32)])
    return {
        'x_prompt': nrm(ks[0], (BATCH, SEQ, D_MODEL), 1.0),
        'x_sample': nrm(ks[1], (DEC_BATCH, DEC_SEQ, D_MODEL), 1.0),
        'p_prompt': nrm(ks[2], (DEPTH, BATCH, SEQ, PLE_DIM), 1.0),
        'p_sample': nrm(ks[3], (DEPTH, DEC_BATCH, DEC_SEQ, PLE_DIM), 1.0),
        'cache_ckv': nrm(ks[4], (DEPTH, DEC_BATCH, PAST_LEN, KV_LORA), 1.0),
        'cache_krope': nrm(ks[5], (DEPTH, DEC_BATCH, PAST_LEN, ROPE_DIM), 1.0),
        'state_hgrn': nrm(ks[6], (DEPTH, DEC_BATCH, HG_HEADS, HG_DK, HG_DV), 0.3),
        'ln0_g': 1.0 + nrm(ks[7], (D_MODEL,), 0.05),
        'ln0_b': nrm(ks[8], (D_MODEL,), 0.02),
        'w_in': nrm(ks[9], (DEPTH, D_MODEL, D_IN), D_MODEL ** -0.5) * col_scale,
        'q_norm': 1.0 + nrm(ks[10], (DEPTH, Q_LORA), 0.05),
        'w_uq': nrm(ks[11], (DEPTH, Q_LORA, MLA_HEADS * (NOPE_DIM + ROPE_DIM)), Q_LORA ** -0.5),
        'kv_norm': 1.0 + nrm(ks[12], (DEPTH, KV_LORA), 0.05),
        'w_uk': nrm(ks[13], (DEPTH, KV_LORA, MLA_HEADS, NOPE_DIM), KV_LORA ** -0.5),
        'w_uv': nrm(ks[14], (DEPTH, KV_LORA, MLA_HEADS, V_DIM), KV_LORA ** -0.5 * DN_BETA),
        'hg_lb': nrm(ks[15], (DEPTH, HG_FDIM), 0.5),
        'hg_norm': 1.0 + nrm(ks[16], (DEPTH, HG_IDIM), 0.05),
        'w_br_a': nrm(ks[17], (DEPTH, MLA_HEADS * V_DIM, D_MODEL), (MLA_HEADS * V_DIM) ** -0.5),
        'w_br_b': nrm(ks[18], (DEPTH, HG_IDIM, D_MODEL), HG_IDIM ** -0.5),
        'w_out': nrm(ks[19], (DEPTH, D_MODEL, D_MODEL), D_MODEL ** -0.5 * DN_BETA),
        'ln1_g': 1.0 + nrm(ks[20], (DEPTH, D_MODEL), 0.05),
        'ln1_b': nrm(ks[21], (DEPTH, D_MODEL), 0.02),
        'w_router_group': nrm(ks[22], (DEPTH, D_MODEL, N_GROUPS), D_MODEL ** -0.5),
        'w_router_expert': nrm(ks[23], (DEPTH, D_MODEL, N_EXPERTS), D_MODEL ** -0.5),
        'w_e_gate': nrm(ks[24], (DEPTH, N_EXPERTS, D_MODEL, D_EXPERT), D_MODEL ** -0.5 * DN_BETA),
        'w_e_up': nrm(ks[25], (DEPTH, N_EXPERTS, D_MODEL, D_EXPERT), D_MODEL ** -0.5 * DN_BETA),
        'w_e_down': nrm(ks[26], (DEPTH, N_EXPERTS, D_EXPERT, D_MODEL), D_EXPERT ** -0.5 * DN_BETA),
        'w_ple': nrm(ks[27], (DEPTH, PLE_DIM, D_MODEL), PLE_DIM ** -0.5),
        'w_ple_gate': nrm(ks[28], (DEPTH, D_MODEL, D_MODEL), D_MODEL ** -0.5),
        'ln2_g': 1.0 + nrm(ks[29], (DEPTH, D_MODEL), 0.05),
        'ln2_b': nrm(ks[30], (DEPTH, D_MODEL), 0.02),
    }

def reference(x_prompt, x_sample, p_prompt, p_sample, cache_ckv, cache_krope, state_hgrn,
              ln0_g, ln0_b, w_in, q_norm, w_uq, kv_norm, w_uk, w_uv, hg_lb, hg_norm,
              w_br_a, w_br_b, w_out, ln1_g, ln1_b, w_router_group, w_router_expert,
              w_e_gate, w_e_up, w_e_down, w_ple, w_ple_gate, ln2_g, ln2_b):
    lbs = hgrn2_lower_bounds(hg_lb)
    xp = layernorm(x_prompt, ln0_g, ln0_b)
    xs = layernorm(x_sample, ln0_g, ln0_b)
    pos_p = jnp.arange(x_prompt.shape[1], dtype=jnp.int32)
    pos_s = PAST_LEN + jnp.arange(x_sample.shape[1], dtype=jnp.int32)
    ckv_p, kr_p, st_p, ckv_s, kr_s, st_s = [], [], [], [], [], []
    for i in range(DEPTH):
        lp = {'w_in': w_in[i], 'q_norm': q_norm[i], 'w_uq': w_uq[i], 'kv_norm': kv_norm[i],
              'w_uk': w_uk[i], 'w_uv': w_uv[i], 'hg_norm': hg_norm[i], 'w_br_a': w_br_a[i],
              'w_br_b': w_br_b[i], 'w_out': w_out[i], 'ln1_g': ln1_g[i], 'ln1_b': ln1_b[i],
              'w_rg': w_router_group[i], 'w_re': w_router_expert[i], 'w1': w_e_gate[i],
              'w3': w_e_up[i], 'w2': w_e_down[i], 'w_ple': w_ple[i], 'w_ple_gate': w_ple_gate[i],
              'ln2_g': ln2_g[i], 'ln2_b': ln2_b[i]}
        xp, c, r, s = trunk_layer(xp, p_prompt[i], pos_p, lp, lbs[i], None)
        ckv_p.append(c)
        kr_p.append(r)
        st_p.append(s)
        xs, c, r, s = trunk_layer(xs, p_sample[i], pos_s, lp, lbs[i], (cache_ckv[i], cache_krope[i], state_hgrn[i]))
        ckv_s.append(c)
        kr_s.append(r)
        st_s.append(s)
    return (xp, xs, jnp.stack(ckv_p), jnp.stack(kr_p), jnp.stack(st_p), jnp.stack(ckv_s), jnp.stack(kr_s), jnp.stack(st_s))


_drawn_inputs = setup_inputs


def setup_inputs(seed=0):
    import zlib

    import numpy as np

    out = dict(_drawn_inputs(seed))
    spreads = {}
    factors = {'cache_ckv': 6.351,
     'cache_krope': 8.0,
     'state_hgrn': 4.406,
     'q_norm': 8.0,
     'w_uq': 3.509,
     'w_uk': 3.925,
     'w_uv': 2.805,
     'hg_norm': 7.498,
     'w_br_a': 2.773}
    for name, (base, spread) in spreads.items():
        noise = np.random.default_rng([zlib.crc32(name.encode()), seed]).standard_normal(out[name].shape)
        drawn = base * np.exp(spread * noise) if base else spread * noise
        out[name] = __import__('jax').numpy.asarray(drawn.astype(out[name].dtype))
    for name, factor in factors.items():
        out[name] = (out[name] * factor).astype(out[name].dtype)
    return out
```

```python
import numpy as np
import concourse.bass as bass
from concourse import mybir
from contextlib import ExitStack

F32 = mybir.dt.float32
I32 = mybir.dt.int32
U32 = mybir.dt.uint32
ALU = mybir.AluOpType
ACT = mybir.ActivationFunctionType
AX = mybir.AxisListType

D = 1024
SEQ, DEC, PAST = 256, 32, 512
DEPTH = 2
CHUNK = 64
HEADS, NOPE, ROPE, VDIM = 8, 64, 32, 64
QK = NOPE + ROPE
QL, KVL = 384, 256
HH, DK = 4, 128
EXPERTS, GROUPS, PER_GROUP = 32, 4, 8
DE = 512
PLE = 256
ALPHA = (2 * DEPTH) ** 0.25
EPS = 1e-6
SCALE = QK ** -0.5
BIG = 1e30
P = 128
NT = [128, 128, 32]
T0 = [0, 128, 256]
T = 288
KEYS = PAST + DEC
LEVELS = 7

RING, SLOT = 8, 2048
QUAD, QUADS, CAP = 4, EXPERTS // 4, 32
MAX_PASS = -(-T // CAP)

C_ID, C_LEV, C_SUF, C_MASK, C_TRI, C_ONE, C_IOTA, C_ROPE = np.cumsum([0, 128, 1024, 128, 1024, 128, 128, 32]).tolist()
C_END = C_ROPE + 3 * 64


def constants():
    c = np.zeros((P, C_END), np.float32)
    u = np.arange(P)[:, None]
    t = np.arange(P)[None, :]
    c[:, C_ID:C_ID + P] = np.eye(P)
    for lv in range(LEVELS):
        m = P >> (lv + 1)
        mid = t // (2 * m) * (2 * m) + m
        right = t >= mid
        c[:, C_LEV + lv * P:C_LEV + (lv + 1) * P] = np.where(right, (u >= mid) & (u <= t), (u > t) & (u < mid))
        same = u // (2 * m) == t // (2 * m)
        c[:, C_MASK + lv * P:C_MASK + (lv + 1) * P] = same & (u % (2 * m) < m) & (t % (2 * m) >= m)
    c[:, C_LEV + LEVELS * P:C_LEV + (LEVELS + 1) * P] = u <= t
    c[:, C_MASK + LEVELS * P:C_MASK + (LEVELS + 1) * P] = u == t
    c[:, C_SUF:C_SUF + P] = u > t
    c[:, C_TRI:C_TRI + P] = u < t
    c[:, C_ONE:C_ONE + P] = 1
    c[:, C_IOTA:C_IOTA + 32] = np.arange(32)
    half = ROPE // 2
    inv = np.float32(10000.0) ** (-np.arange(half, dtype=np.float32) / np.float32(half))
    for i in range(3):
        pos = (np.arange(P) + (T0[i] if i < 2 else PAST)).astype(np.float32)
        ang = pos[:, None] * inv[None, :].astype(np.float32)
        cs, sn = np.cos(ang), np.sin(ang)
        c[:, C_ROPE + 64 * i:C_ROPE + 64 * (i + 1)] = np.concatenate([cs, cs, -sn, sn], 1)
    return c


def mask_rows():
    r = np.zeros((2, 2, SEQ), np.float32)
    for i in range(2):
        r[0, i, 2 * i * CHUNK:(2 * i + 1) * CHUNK] = 1.0
        r[1, i, (2 * i + 1) * CHUNK:(2 * i + 2) * CHUNK] = -BIG
    return r


def weight_pieces():
    out = []
    for name in ("cq", "kv", "f", "q", "i", "g"):
        out += [(name, 0), (name, 1)]
    out += [("uq", 0), ("uq", 1), ("uk", 0), ("uv", 0)]
    for j in range(2):
        out += [("ga", j, 0), ("ga", j, 1), ("bra", j), ("gb", j, 0), ("gb", j, 1), ("brb", j)]
    out += [("wo", j, h) for j in range(2) for h in range(2)]
    out += [("pg", j, h) for j in range(2) for h in range(2)]
    out += [("pl",)]
    return out


PIECES = weight_pieces()
MOE_PIECES = [(w, h, e) for w in ("eg", "eu", "ed") for h in range(2) for e in range(QUAD)]
LAYER_PIECES = len(PIECES) + QUADS * len(MOE_PIECES)
OFF = dict(cq=(0, 384), kv=(384, 672), f=(672, 1184), q=(1184, 1696), i=(1696, 2208), g=(2208, 2720),
           ga=(2720, 3744), gb=(3744, 4768))


def tensor_jobs():
    j = [("tx", t, h) for t in range(3) for h in range(2)]
    for name in ("cq", "kv", "f", "q", "i", "g"):
        j += [(name, t) for t in range(3)]
    j += [("cT", t) for t in range(3)] + [("kvT", t) for t in range(3)]
    j += [("uq", t, h) for h in range(2) for t in range(3)]
    j += [("kT", i) for i in range(4)] + [("V", t) for t in range(2)]
    j += [("qT", t, h) for t in range(2) for h in range(2)] + [("qTs",)]
    for i in range(2):
        j += [("S", i, n) for n in range(2 + 2 * i)]
        j += [("PT", i, kt, h) for kt in range(i + 1) for h in range(2)]
        j += [("aT", i)]
    j += [("cc", k) for k in range(4)] + [("wuT", i) for i in range(4)] + [("ql",)]
    j += [("ss", 0), ("ss", 1), ("ss", 2)] + [("PTs", i) for i in range(3)] + [("lat",), ("aTs",)]
    for t in range(3):
        nb = 2 if t < 2 else 1
        j += [("hq", t), ("hk", t), ("suf", t)]
        j += [("E", t, 0, b) for b in range(nb)]
        for h in range(HH):
            if h < HH - 1:
                j += [("E", t, h + 1, b) for b in range(nb)]
            j += [("A", t, h, b) for b in range(nb)]
        j += [("o", t), ("Sn", t), ("oT", t)]
    for n in range(2):
        for w in ("ga", "bra", "gb", "brb"):
            j += [(w, n, t) for t in range(3)]
    j += [("mT", t, h) for t in range(3) for h in range(2)]
    j += [("wo", n, t) for n in range(2) for t in range(3)]
    j += [("t1", t, h) for t in range(3) for h in range(2)]
    j += [("rt", t) for t in range(3)] + [("pT", t) for t in range(3)]
    for n in range(2):
        j += [("pg", n, t) for t in range(3)]
    j += [("pl", n, t) for n in range(2) for t in range(3)]
    j += [("rk", t) for t in range(3)] + [("cnt",)]
    return j


JOBS = tensor_jobs()
MOE_JOBS = [("X", 0), ("X", 1), ("ST",), ("G",), ("U",), ("hT",), ("Y", 0), ("Y", 1)] + \
    [("C", t, j) for t in range(3) for j in range(2)]
MOE_BANK = [0, 1, 5, 2, 3, 4, 6, 7, 0, 1, 2, 3, 4, 5]
BANKS = 8


class Book:

    def __init__(self):
        self.at = {}
        n, uses = 0, [0] * BANKS
        self.moe_uses = [MOE_BANK.count(b) for b in range(BANKS)]
        for layer in range(DEPTH):
            for k, job in enumerate(JOBS):
                b = k % BANKS
                self.at[(layer,) + job] = (n, b, uses[b])
                n += 1
                uses[b] += 1
            seen = [0] * BANKS
            for k, job in enumerate(MOE_JOBS):
                b = MOE_BANK[k]
                self.at[(layer, "moe") + job] = (n + k, b, uses[b] + seen[b])
                seen[b] += 1
            n += QUADS * len(MOE_JOBS)
            uses = [a + QUADS * m for a, m in zip(uses, self.moe_uses)]

    def number(self, key, g=0):
        return self.at[key][0] + 1 + (g * len(MOE_JOBS) if key[1] == "moe" else 0)

    def bank(self, key):
        return self.at[key][1]

    def uses(self, key, g=0):
        return self.at[key][2] + (g * self.moe_uses[self.at[key][1]] if key[1] == "moe" else 0)


class Steps:

    def __init__(self, eng, sem):
        self.eng, self.sem, self.n, self.per, self.g = eng, sem, 0, 0, None

    def step(self, ins):
        self.n += 1
        ins.then_inc(self.sem, 1)
        self.eng.wait_ge(self.sem, self.n if self.g is None else self.n + self.g * self.per)

    def enter(self, per):
        self.per, self.first = per, self.n

    def leave(self, turns):
        assert self.n - self.first == self.per, (self.n - self.first, self.per)
        self.n, self.g = self.first + turns * self.per, None


def last_use(key):
    name = key[0]
    if name in ("cq", "kv", "f", "q", "i", "g"):
        return (name, 2)
    if name == "uq":
        return ("uq", 2, key[1])
    if name in ("uk", "uv"):
        return ("aTs",)
    if name == "pl":
        return ("pl", 1, 2)
    return (name, key[1], 2)


def piece_number(layer, key):
    return layer * LAYER_PIECES + PIECES.index(key)


def build(nc, x_prompt, x_sample, p_prompt, p_sample, cache_ckv, cache_krope, state_hgrn,
          ln0_g, ln0_b, w_in, q_norm, w_uq, kv_norm, w_uk, w_uv, hg_lb, hg_norm,
          w_br_a, w_br_b, w_out, ln1_g, ln1_b, w_router_group, w_router_expert,
          w_e_gate, w_e_up, w_e_down, w_ple, w_ple_gate, ln2_g, ln2_b, consts, masks,
          y_prompt, y_sample, ckv_p, krope_p, state_p, ckv_s, krope_s, state_s):
    book = Book()
    ctx = ExitStack()
    with ctx:
        def sb(name, cols, dt=F32):
            return ctx.enter_context(nc.sbuf_tensor(name, [P, cols], dt))

        def sem(name):
            return ctx.enter_context(nc.semaphore(name))

        ring = sb("ring", RING * SLOT)
        cst = sb("cst", C_END)
        x = sb("x_sb", 3 * D)[:, :].rearrange("p (t d) -> p t d", t=3)
        xT = sb("xT", 8 * T)[:, :].rearrange("p (c t) -> p c t", c=8)
        lnw = sb("lnw", 2 * D)[:, :].rearrange("p (k d) -> p k d", k=2)
        nrm = sb("nrm", QL + KVL + HH * DK)
        qn_row, kn_row, hn_row = nrm[:, 0:QL], nrm[:, QL:QL + KVL], nrm[:, QL + KVL:QL + KVL + 512]
        lb = sb("lb", 3 * 512)[:, :].rearrange("p (k d) -> p k d", k=3)
        ln_lb, ln_1mlb, one_mlb = lb[:, 0, :], lb[:, 1, :], lb[:, 2, :]
        wr = sb("wr", 8 * 36)[:, :].rearrange("p (c n) -> p c n", c=8)
        sm = sb("small", 256)
        arena = sb("arena", 22112)

        def carve(start, *shape):
            n = int(np.prod(shape))
            assert start + n <= 22112
            a = arena[:, start:start + n]
            if len(shape) == 2:
                return a.rearrange("p (a b) -> p a b", a=shape[0])
            if len(shape) == 3:
                return a.rearrange("p (a b c) -> p a b c", a=shape[0], b=shape[1])
            return a

        cq = carve(0, 3, QL)
        cqT = carve(1152, 3, T)
        q = carve(2016, 3, HEADS * QK)
        prob = carve(0, HEADS, 256)
        probT = carve(2048, 2, HEADS, 128)
        prob_s = carve(0, 2, KEYS)
        probT_s = carve(1088, 5, 256)
        Y = 4320
        qT = carve(Y, HEADS, 256)
        qTs = carve(Y + 2048, HEADS, 32)
        ckv = carve(Y + 2304, 3, KVL)
        ckvT = carve(Y + 3072, 2, T)
        krp = carve(Y + 3648, 3, QK)
        kT = carve(Y + 3936, HEADS, 256)
        fw = carve(Y + 3936, 3, 512)
        val = carve(Y + 5984, 2, 512)
        wukT = carve(Y + 3936, HEADS, 2, 128)
        qlatT = carve(Y + 5984, 2, 256)
        latT = carve(Y + 6496, 2, 256)
        cT = carve(Y, 2, KEYS)
        Z = Y + 7008
        cache = carve(Z, 4, KVL)
        krc = carve(Z + 1024, 4, QK)
        kcT = carve(Z + 1408, KEYS)
        AT = Z + 1952
        aT = carve(AT, 4, T)
        H = AT + 1152
        lf = carve(H, 3, 512)
        hk = carve(H + 1536, 3, 512)
        hq = carve(H + 3072, 3, 512)
        hv = carve(H + 4608, 3, 512)
        hg = carve(H + 6144, 3, 512)
        dec = [carve(i * 1024, 1024) for i in range(2)]
        qh = [carve(2048 + i * 1024, 1024) for i in range(2)]
        kh = [carve(4096 + i * 1024, 1024) for i in range(2)]
        am = [carve(6144 + i * 1024, 1024) for i in range(2)]
        hqT = carve(8192, HH, 128)
        hkT = carve(8704, HH, 128)
        qcum = carve(9216, HH, 128)
        osb = carve(9728, 512)
        oT = carve(10240, 4, T)
        state = [carve(11392, HH, DK), carve(11904, HH, DK)]
        att = carve(12416, HH, 128)
        mg = carve(H, 3, D)
        gate_a = carve(H + 3072, 3, 512)
        gate_b = carve(H + 4608, 3, 512)
        mT = xT
        acc = carve(0, 3, D)
        pin = carve(3072, 3, PLE)
        pT = carve(3840, 2, T)
        pgate = carve(4416, 3, D)
        rl = carve(7488, 3, 64)
        onehot = carve(7680, 3, 64)
        route = carve(7872, 3, 32)
        rsm = carve(8064, 3, 64)
        sel = carve(8352, 3, 128)
        selw = carve(8736, 3, 128)
        selT = carve(9120, T)
        posm = carve(12992, 3, 36)
        wsel = carve(13104, 3, 36)
        xeT = carve(9408, 8, 128)
        eh = carve(10432, 512)
        hid = carve(10944, 512)
        hidT = carve(11456, 4, 128)
        ye = carve(11968, D)
        extra_w = [carve(13312 + i * SLOT, SLOT) for i in range(QUAD)]
        cst_c = cst[:, :]
        counts = sb("counts", 16, I32)
        rtmp = sb('rtmp', HEADS * 64)[:, :].rearrange('p (h c) -> p h c', h=HEADS)
        lbtmp = rtmp[:, :, :].rearrange('p h c -> p (h c)')

        ident = cst[:, C_ID:C_ID + P]
        levs = cst[:, C_LEV:C_LEV + 1024].rearrange("p (l t) -> p l t", l=8)
        maskc = cst[:, C_MASK:C_MASK + 1024].rearrange("p (l t) -> p l t", l=8)
        suf = cst[:, C_SUF:C_SUF + P]
        tri = cst[:, C_TRI:C_TRI + P]
        ones = cst[:, C_ONE:C_ONE + P]
        iota = cst[:, C_IOTA:C_IOTA + 32]

        eps_col = sm[:, 0:1]
        ssq = sm[:, 1:4]
        ln_st = sm[:, 4:16]
        ln_mv = sm[:, 16:18]
        ln_rs = sm[:, 18:21]
        ln_nm = sm[:, 21:24]
        ssk = sm[:, 24:27]
        mx = sm[:, 32:48]
        nb = sm[:, 48:64]
        psum_ = sm[:, 64:80]
        prec = sm[:, 80:96]
        oss = sm[:, 96:108]
        mvs = sm[:, 108:114]
        bend = sm[:, 116:128]

        banks = [ctx.enter_context(nc.psum_tensor(f"bank{b}", [P, 512], F32)) for b in range(BANKS)]

        ring_full = [sem(f"ring_full{i}") for i in range(RING)]
        halves_used = sem("halves_used")
        matmuls_done = sem("matmuls_done")
        bank_emptied = [sem(f"bank_emptied{b}") for b in range(BANKS)]
        consts_in = sem("consts_in")
        x_in = sem("x_in")
        lnw_in = sem("lnw_in")
        rows_in = sem("rows_in")
        mask_in = sem("mask_in")
        cache_in = sem("cache_in")
        state_in = sem("state_in")
        ple_in = sem("ple_in")
        lb_in = sem("lb_in")
        stored = sem("stored")
        eps_set = sem("eps_set")
        zeroed = sem("zeroed")
        vec_step = sem("vec_step")
        act_step = sem("act_step")
        ln_var = sem("ln_var")
        ln_rstd = sem("ln_rstd")
        ln_out = sem("ln_out")
        lat_rstd = sem("lat_rstd")
        f_act = sem("f_act")
        f_gap = sem("f_gap")
        f_add = sem("f_add")
        silu_e = sem("silu_e")
        kr_out = sem("kr_out")
        q_out = sem("q_out")
        nmax = sem("nmax")
        prob_out = sem("prob_out")
        lf_out = sem("lf_out")
        hk_out = sem("hk_out")
        qh_out = sem("qh_out")
        kh_out = sem("kh_out")
        att_out = sem("att_out")
        ksuf_out = sem("ksuf_out")
        o_sq = sem("o_sq")
        o_out = sem("o_out")
        gate_e = sem("gate_e")
        mg_out = sem("mg_out")
        x_mix = sem("x_mix")
        route_e = sem("route_e")
        route_v = sem("route_v")
        route_out = sem("route_out")
        pos_out = sem("pos_out")
        pgate_e = sem("pgate_e")
        sel_out = sem("sel_out")
        prob_s_out = sem("prob_s_out")
        smax_s = sem("smax_s")
        eh_out = sem("eh_out")
        lb_e = sem("lb_e")
        lb_v = sem("lb_v")
        counts_out = sem("counts_out")
        more_chosen = sem("more_chosen")
        more_weights = sem("more_weights")
        more_matmuls = sem("more_matmuls")
        more_exp = sem("more_exp")
        more_read = sem("more_read")

        block = ctx.enter_context(nc.Block())

        def job_done(eng, key, g=0):
            eng.wait_ge(matmuls_done, book.number(key, g))

        def job_read(eng, key, g=0):
            eng.wait_ge(bank_emptied[book.bank(key)], book.uses(key, g) + 1)

        def emptied(ins, key):
            return ins.then_inc(bank_emptied[book.bank(key)], 1)

        def bank(key):
            return banks[book.bank(key)]

        def further_passes(eng, layer, turn, body, each_pass=None):
            eng.wait_ge(counts_out, layer + 1)
            fullest = eng.value_load(counts[0:1, 0:1], min_val=0, max_val=T)
            with eng.If(fullest > CAP):
                with eng.Fori(1, MAX_PASS) as k:
                    if each_pass:
                        each_pass()
                    with eng.Fori(0, QUADS) as g:
                        tokens = eng.value_load(counts[0:1, bass.ds(g + 1, 1)], min_val=0, max_val=T)
                        with eng.If(tokens > k * CAP):
                            body(g, eng.snap(turn))
                            eng.reg_add(turn, turn, 1)

        def slot(n):
            return ring[:, (n % RING) * SLOT:(n % RING + 1) * SLOT]

        def bcast(ap, axis, n):
            a = ap.unsqueeze(axis)
            shape = list(a.shape)
            shape[axis] = n
            return a.broadcast_to(shape)

        @block.sync
        def _(sp):
            def wait_used(n, g=0):
                layer, k = divmod(n, LAYER_PIECES)
                if k < len(PIECES):
                    job_done(sp, (layer,) + last_use(PIECES[k]))
                    return
                quad, i = divmod(k - len(PIECES), len(MOE_PIECES))
                w, h, _ = MOE_PIECES[i]
                if h == 0:
                    order = ("eg", "eu", "ed").index(w) + 1
                    sp.wait_ge(halves_used, 3 * (QUADS * layer + quad) + order + g * 3)
                else:
                    job_done(sp, (layer, "moe") + dict(eg=("G",), eu=("U",), ed=("Y", 1))[w], g + quad)

            def load(n, c, cols, src, g=0):
                if n >= RING:
                    wait_used(n - RING, g)
                dst = slot(n)[:, 0:c * cols].rearrange("p (c n) -> p c n", c=c)
                sp.dma_start(dst, src).then_inc(ring_full[n % RING], 16)

            for layer in range(DEPTH):
                win = w_in[layer].rearrange("(p c) n -> p c n", c=8)
                for key in PIECES:
                    n = piece_number(layer, key)
                    name = key[0]
                    if name in ("cq", "kv", "f", "q", "i", "g"):
                        a, b = OFF[name]
                        load(n, 4, b - a, win[:, 4 * key[1]:4 * key[1] + 4, a:b])
                    elif name in ("ga", "gb"):
                        a = OFF[name][0] + 512 * key[1]
                        load(n, 4, 512, win[:, 4 * key[2]:4 * key[2] + 4, a:a + 512])
                    elif name == "uq":
                        load(n, 3, 384, w_uq[layer].rearrange("(p c) n -> p c n", c=3)[:, :, 384 * key[1]:384 * key[1] + 384])
                    elif name in ("uk", "uv"):
                        w = w_uk if name == "uk" else w_uv
                        load(n, 2, 512, w[layer].rearrange("(p c) h n -> p c (h n)", c=2))
                    elif name in ("bra", "brb"):
                        w = w_br_a if name == "bra" else w_br_b
                        load(n, 4, 512, w[layer].rearrange("(c p) n -> p c n", p=P)[:, :, 512 * key[1]:512 * key[1] + 512])
                    elif name in ("wo", "pg"):
                        w = w_out if name == "wo" else w_ple_gate
                        v = w[layer].rearrange("(p c) n -> p c n", c=8)
                        load(n, 4, 512, v[:, 4 * key[2]:4 * key[2] + 4, 512 * key[1]:512 * key[1] + 512])
                    else:
                        load(n, 2, D, w_ple[layer].rearrange("(p c) n -> p c n", c=2))
                first = layer * LAYER_PIECES + len(PIECES)
                experts = dict(eg=w_e_gate[layer].rearrange("e (p h c) n -> e p h (c n)", p=P, h=2),
                               eu=w_e_up[layer].rearrange("e (p h c) n -> e p h (c n)", p=P, h=2),
                               ed=w_e_down[layer].rearrange("e (p h c) n -> e p h (c n)", p=P, h=2))
                for i, (w, h, e) in enumerate(MOE_PIECES):
                    load(first + i, 1, SLOT, experts[w][e:e + 1, :, h, :].rearrange("e p n -> p e n"))
                with sp.Fori(0, QUADS - 1) as g:
                    for i, (w, h, e) in enumerate(MOE_PIECES):
                        src = experts[w][bass.ds(g * QUAD + (QUAD + e), 1), :, h, :].rearrange("e p n -> p e n")
                        load(first + len(MOE_PIECES) + i, 1, SLOT, src, g)

        @block.gpsimd
        def _(pool):
            pool.memset(sm[:, :], 0.0).then_inc(zeroed, 1)
            pool.wait_ge(zeroed, 1)
            pool.memset(eps_col, EPS).then_inc(eps_set, 1)
            pool.dma_start(cst_c, consts).then_inc(consts_in, 16)
            for t in range(3):
                src = x_prompt[0, T0[t]:T0[t] + P, :] if t < 2 else x_sample[0]
                pool.dma_start(x[0:NT[t], t, :], src).then_inc(x_in, 16)

            def load_ln(k, g_row, b_row):
                if k:
                    pool.wait_ge(ln_out, 3 * k)
                pool.dma_start(lnw[:, 0, :], g_row.partition_broadcast(P)).then_inc(lnw_in, 16)
                pool.dma_start(lnw[:, 1, :], b_row.partition_broadcast(P)).then_inc(lnw_in, 16)

            load_ln(0, ln0_g, ln0_b)
            for layer in range(DEPTH):
                if layer:
                    pool.wait_ge(ln_out, 3 * (1 + 2 * layer))
                pool.dma_start(qn_row, q_norm[layer].partition_broadcast(P)).then_inc(rows_in, 16)
                pool.dma_start(kn_row, kv_norm[layer].partition_broadcast(P)).then_inc(rows_in, 16)
                pool.dma_start(hn_row, hg_norm[layer].partition_broadcast(P)).then_inc(rows_in, 16)
                pool.dma_start(wr[:, :, 0:4], w_router_group[layer].rearrange("(p c) n -> p c n", c=8)).then_inc(rows_in, 16)
                pool.dma_start(wr[:, :, 4:36], w_router_expert[layer].rearrange("(p c) n -> p c n", c=8)).then_inc(rows_in, 16)
                pool.dma_start(cache[:, :, :], cache_ckv[layer, 0].rearrange("(t p) c -> p t c", p=P)).then_inc(cache_in, 16)
                pool.memset(krc[:, :, 0:NOPE], 0.0).then_inc(zeroed, 1)
                pool.dma_start(krc[:, :, NOPE:QK], cache_krope[layer, 0].rearrange("(t p) c -> p t c", p=P)).then_inc(cache_in, 16)
                pool.memset(krp[:, :, 0:NOPE], 0.0).then_inc(zeroed, 1)
                if layer == 1:
                    for k in range(2):
                        pool.dma_start(fw[:, k, :], hg_lb[k].partition_broadcast(P)).then_inc(lb_in, 16)
                load_ln(1 + 2 * layer, ln1_g[layer], ln1_b[layer])
                for t in range(3):
                    job_read(pool, (layer, "kv", t))
                    dst = ckv_p[layer, 0, T0[t]:T0[t] + P, :] if t < 2 else ckv_s[layer, 0]
                    pool.dma_start(dst, ckv[0:NT[t], t, :]).then_inc(stored, 16)
                    pool.wait_ge(kr_out, 3 * layer + t + 1)
                    dst = krope_p[layer, 0, T0[t]:T0[t] + P, :] if t < 2 else krope_s[layer, 0]
                    pool.dma_start(dst, krp[0:NT[t], t, NOPE:QK]).then_inc(stored, 16)
                pool.wait_ge(lf_out, 3 * layer + 3)
                for h in range(HEADS):
                    pool.dma_start(qT[QK:QK + 2, h, :], masks[0]).then_inc(mask_in, 16)
                    pool.dma_start(kT[QK:QK + 2, h, :], masks[1]).then_inc(mask_in, 16)
                job_read(pool, (layer, "aTs"))
                pool.memset(state[0][:, :, :], 0.0).then_inc(zeroed, 1)
                pool.dma_start(state[1][:, :, :], state_hgrn[layer, 0].rearrange("h k v -> k h v")).then_inc(state_in, 16)
                for i in range(2):
                    job_read(pool, (layer, "Sn", 1 + i))
                    dst = (state_p if i == 0 else state_s)[layer, 0].rearrange("h k v -> k h v")
                    pool.dma_start(dst, state[i][:, :, :]).then_inc(stored, 16)
                job_read(pool, (layer, "oT", 2))
                for t in range(3):
                    src = p_prompt[layer, 0, T0[t]:T0[t] + P, :] if t < 2 else p_sample[layer, 0]
                    pool.dma_start(pin[0:NT[t], t, :], src).then_inc(ple_in, 16)
                load_ln(2 + 2 * layer, ln2_g[layer], ln2_b[layer])
                pool.wait_ge(stored, 16 * 8 * (layer + 1))
            pool.wait_ge(ln_out, 3 * (1 + 2 * DEPTH))
            for t in range(3):
                dst = y_prompt[0, T0[t]:T0[t] + P, :] if t < 2 else y_sample[0]
                pool.dma_start(dst, x[0:NT[t], t, :]).then_inc(stored, 16)
            pool.wait_ge(stored, 16 * (8 * DEPTH + 3))

        @block.tensor
        def _(pe):
            def open_bank(key, g=0):
                if book.at[key][2]:
                    pe.wait_ge(bank_emptied[book.bank(key)], book.uses(key, g))
                return bank(key)

            def arrived(n, g=0):
                per = len(MOE_PIECES) // RING
                pe.wait_ge(ring_full[n % RING], 16 * (n // RING + 1) + g * (16 * per))

            def done(ins, n=1):
                return ins.then_inc(matmuls_done, n)

            def mm(out, lhsT, rhs, first, last):
                return pe.matmul(out, lhsT, rhs, start=first, stop=last, skip_group_check=True)

            def project(layer, key, tiles, lhs, width, names):
                ns = [piece_number(layer, nm) for nm in names]
                for n in ns:
                    arrived(n)
                for t in tiles:
                    b = open_bank((layer,) + key + (t,))
                    k = 0
                    for n in ns:
                        w = slot(n)[:, 0:4 * width].rearrange("p (c n) -> p c n", c=4)
                        for c in range(4):
                            ins = mm(b[0:NT[t], 0:width], lhs[:, k, T0[t]:T0[t] + NT[t]], w[:, c, :], k == 0,
                                     k == 4 * len(ns) - 1)
                            k += 1
                    done(ins)

            def transposes(layer, key, parts, wait=None):
                b = open_bank((layer,) + key)
                for a, m, src in parts:
                    ins = pe.transpose(b[0:m, a:a + src.shape[0]], src, ident[0:src.shape[0], 0:src.shape[0]])
                done(ins)

            turn = pe.alloc_register("pe_turn")
            pe.reg_mov(turn, 0)
            pe.sem_inc(more_matmuls, 1)
            pe.wait_ge(consts_in, 16)
            pe.wait_ge(eps_set, 1)
            for layer in range(DEPTH):
                for t in range(3):
                    pe.wait_ge(ln_out, 3 * 2 * layer + t + 1)
                    for h in range(2):
                        transposes(layer, ("tx", t, h), [((c % 4) * P, P, x[0:NT[t], t, c:D:8]) for c in range(4 * h, 4 * h + 4)])
                for t in range(3):
                    for h in range(2):
                        job_read(pe, (layer, "tx", t, h))
                for name in ("cq", "kv", "f", "q", "i", "g"):
                    project(layer, (name,), range(3), xT, OFF[name][1] - OFF[name][0], [(name, 0), (name, 1)])
                for t in range(3):
                    job_read(pe, (layer, "cq", t))
                    pe.wait_ge(kr_out, 3 * layer + t + 1)
                    n = NT[t]
                    transposes(layer, ("cT", t), [(c * P, P, cq[0:n, t, c:QL:3]) for c in range(3)]
                               + [(3 * P, QK, krp[0:n, t, :])])
                for t in range(3):
                    job_read(pe, (layer, "kv", t))
                    transposes(layer, ("kvT", t), [(c * P, P, ckv[0:NT[t], t, c:KVL:2]) for c in range(2)])
                for t in range(3):
                    job_read(pe, (layer, "cT", t))
                for h in range(2):
                    n = piece_number(layer, ("uq", h))
                    arrived(n)
                    w = slot(n)[:, 0:1152].rearrange("p (c n) -> p c n", c=3)
                    for t in range(3):
                        b = open_bank((layer, "uq", t, h))
                        for c in range(3):
                            ins = mm(b[0:NT[t], 0:384], cqT[:, c, T0[t]:T0[t] + NT[t]], w[:, c, :], c == 0, c == 2)
                        done(ins)
                nk, nv = piece_number(layer, ("uk", 0)), piece_number(layer, ("uv", 0))
                arrived(nk)
                arrived(nv)
                wk = slot(nk)[:, 0:1024].rearrange("p (c n) -> p c n", c=2)
                wv = slot(nv)[:, 0:1024].rearrange("p (c n) -> p c n", c=2)
                for t in range(3):
                    job_read(pe, (layer, "kvT", t))
                for i in range(4):
                    b = open_bank((layer, "kT", i))
                    for h in (2 * i, 2 * i + 1):
                        for c in range(2):
                            ins = mm(b[0:NOPE, (h % 2) * 256:(h % 2) * 256 + 256], wk[:, c, h * NOPE:(h + 1) * NOPE],
                                     ckvT[:, c, 0:SEQ], c == 0, c == 1)
                    done(ins)
                for t in range(2):
                    b = open_bank((layer, "V", t))
                    for c in range(2):
                        ins = mm(b[:, :], ckvT[:, c, T0[t]:T0[t] + P], wv[:, c, :], c == 0, c == 1)
                    done(ins)
                for t in range(2):
                    pe.wait_ge(q_out, 3 * layer + t + 1)
                    for h in range(2):
                        transposes(layer, ("qT", t, h), [(k * P, QK, q[:, t, (4 * h + k) * QK:(4 * h + k + 1) * QK]) for k in range(4)])
                pe.wait_ge(q_out, 3 * layer + 3)
                transposes(layer, ("qTs",), [(h * DEC, QK, q[0:DEC, 2, h * QK:(h + 1) * QK]) for h in range(HEADS)])
                for i in range(4):
                    job_read(pe, (layer, "kT", i))
                pe.wait_ge(mask_in, 256 * (layer + 1))
                for i in range(2):
                    nkeys = P * (i + 1)
                    per = 512 // nkeys
                    for h in range(2):
                        job_read(pe, (layer, "qT", i, h))
                    for n in range(HEADS // per):
                        b = open_bank((layer, "S", i, n))
                        for k in range(per):
                            h = n * per + k
                            ins = mm(b[:, k * nkeys:(k + 1) * nkeys], qT[0:QK + 2, h, T0[i]:T0[i] + P],
                                     kT[0:QK + 2, h, 0:nkeys], True, True)
                        done(ins)
                    pe.wait_ge(prob_out, 6 * layer + (2 if i == 0 else 6))
                    for kt in range(i + 1):
                        for h in range(2):
                            transposes(layer, ("PT", i, kt, h),
                                       [(k * P, P, prob[:, 4 * h + k, kt * P:(kt + 1) * P]) for k in range(4)])
                    for kt in range(i + 1):
                        job_read(pe, (layer, "V", kt))
                        for h in range(2):
                            job_read(pe, (layer, "PT", i, kt, h))
                    b = open_bank((layer, "aT", i))
                    for c in range(4):
                        for kt in range(i + 1):
                            for h in (2 * c, 2 * c + 1):
                                r = 64 * (h % 2)
                                ins = mm(b[r:r + 64, c * P:(c + 1) * P], val[:, kt, h * VDIM:(h + 1) * VDIM],
                                         probT[:, kt, h, :], kt == 0, kt == i)
                    done(ins)
                pe.wait_ge(cache_in, 32 * (layer + 1))
                pe.wait_ge(zeroed, 3 * layer + 3)
                for k in range(4):
                    transposes(layer, ("cc", k), [(c * P, P, cache[:, k, c:KVL:2]) for c in range(2)] + [(256, QK, krc[:, k, :])])
                for i in range(4):
                    transposes(layer, ("wuT", i), [((2 * (h % 2) + c) * P, NOPE, wk[:, c, h * NOPE:(h + 1) * NOPE])
                                                   for h in (2 * i, 2 * i + 1) for c in range(2)])
                for i in range(4):
                    job_read(pe, (layer, "wuT", i))
                job_read(pe, (layer, "qTs"))
                b = open_bank((layer, "ql"))
                for c in range(2):
                    for h in range(HEADS):
                        ins = mm(b[:, c * 256 + h * DEC:c * 256 + (h + 1) * DEC], wukT[0:NOPE, h, c, :], qTs[0:NOPE, h, :], True, True)
                done(ins)
                for k in range(4):
                    job_read(pe, (layer, "cc", k))
                job_read(pe, (layer, "ql"))
                qs = qTs[0:QK, :, :].rearrange("p h q -> p (h q)")
                for r in range(2):
                    b = open_bank((layer, "ss", r))
                    for c in range(2):
                        mm(b[:, 0:PAST], qlatT[:, c, r * P:(r + 1) * P], cT[:, c, 0:PAST], c == 0, False)
                    done(mm(b[:, 0:PAST], qs[:, r * P:(r + 1) * P], kcT[0:QK, 0:PAST], False, True))
                b = open_bank((layer, "ss", 2))
                for r in range(2):
                    for c in range(2):
                        mm(b[:, r * DEC:(r + 1) * DEC], qlatT[:, c, r * P:(r + 1) * P], ckvT[:, c, T0[2]:T], c == 0, False)
                    ins = mm(b[:, r * DEC:(r + 1) * DEC], qs[:, r * P:(r + 1) * P], kcT[0:QK, PAST:KEYS], False, True)
                done(ins)
                pe.wait_ge(prob_s_out, 2 * (layer + 1))
                for i in range(3):
                    tiles = (2 * i, 2 * i + 1) if i < 2 else (4,)
                    parts = []
                    for kt in tiles:
                        n = min(P, KEYS - kt * P)
                        parts += [((kt % 2) * 256 + r * P, n, prob_s[:, r, kt * P:kt * P + n]) for r in range(2)]
                    transposes(layer, ("PTs", i), parts)
                for i in range(3):
                    job_read(pe, (layer, "PTs", i))
                b = open_bank((layer, "lat"))
                for c in range(2):
                    for kt in range(5):
                        lhs = cache[:, kt, c:KVL:2] if kt < 4 else ckv[0:DEC, 2, c:KVL:2]
                        ins = mm(b[:, c * 256:(c + 1) * 256], lhs, probT_s[0:lhs.shape[0], kt, :], kt == 0, kt == 4)
                done(ins)
                job_read(pe, (layer, "lat"))
                b = open_bank((layer, "aTs"))
                for h in range(HEADS):
                    r = 64 * (h % 2)
                    for c in range(2):
                        ins = mm(b[r:r + 64, (h // 2) * DEC:(h // 2 + 1) * DEC], wv[:, c, h * VDIM:(h + 1) * VDIM],
                                 latT[:, c, h * DEC:(h + 1) * DEC], c == 0, c == 1)
                done(ins)
                job_read(pe, (layer, "aTs"))
                for t in range(3):
                    n = NT[t]
                    nb = 2 if t < 2 else 1
                    lo = 0 if t < 2 else 2
                    pe.wait_ge(hk_out, 3 * layer + t + 1)
                    job_read(pe, (layer, "q", t))
                    pe.wait_ge(lf_out, 3 * layer + t + 1)
                    transposes(layer, ("hq", t), [(h * P, DK, hq[0:n, t, h * DK:(h + 1) * DK]) for h in range(HH)])
                    transposes(layer, ("hk", t), [(h * P, DK, hk[0:n, t, h * DK:(h + 1) * DK]) for h in range(HH)])
                    b = open_bank((layer, "suf", t))
                    done(mm(b[0:n, :], suf[0:n, 0:n], lf[0:n, t, :], True, True))

                    def sums(h):
                        for k in range(nb):
                            b = open_bank((layer, "E", t, h, k))
                            if nb == 2:
                                rhs, w = levs[:, 4 * k:4 * k + 4, :], 512
                            else:
                                rhs, w = levs[0:n, lo:8, 0:n], (8 - lo) * n
                            done(mm(b[:, 0:w], lf[0:n, t, h * DK:(h + 1) * DK], rhs, True, True))

                    sums(0)
                    job_read(pe, (layer, "hq", t))
                    job_read(pe, (layer, "hk", t))
                    for h in range(HH):
                        if h < HH - 1:
                            sums(h + 1)
                        at = (3 * layer + t) * HH + h + 1
                        pe.wait_ge(qh_out, at)
                        pe.wait_ge(kh_out, at)
                        for k in range(nb):
                            b = open_bank((layer, "A", t, h, k))
                            blocks = range(4 * k, 4 * k + 4) if nb == 2 else range(8 - lo)
                            for i, blk in enumerate(blocks):
                                if blk == 7 - lo:
                                    kk, qq = hkT[:, h, 0:n], hqT[:, h, 0:n]
                                else:
                                    kk, qq = kh[h % 2][:, blk * n:(blk + 1) * n], qh[h % 2][:, blk * n:(blk + 1) * n]
                                ins = mm(b[0:n, i * n:(i + 1) * n], kk, qq, True, True)
                            done(ins)
                    if t == 0:
                        pe.wait_ge(zeroed, 3 * layer + 4)
                    elif t == 1:
                        job_read(pe, (layer, "Sn", 0))
                    else:
                        pe.wait_ge(state_in, 16 * (layer + 1))
                    pe.wait_ge(att_out, (3 * layer + t + 1) * HH)
                    st = state[0 if t < 2 else 1]
                    b = open_bank((layer, "o", t))
                    for h in range(HH):
                        c = slice(h * DK, (h + 1) * DK)
                        mm(b[0:n, c], att[0:n, h, 0:n], hv[0:n, t, c], True, False)
                        ins = mm(b[0:n, c], qcum[:, h, 0:n], st[:, h, :], False, True)
                    done(ins)
                    pe.wait_ge(ksuf_out, 3 * layer + t + 1)
                    b = open_bank((layer, "Sn", t))
                    for h in range(HH):
                        c = slice(h * DK, (h + 1) * DK)
                        ins = mm(b[:, c], hk[0:n, t, c], hv[0:n, t, c], True, True)
                    done(ins)
                    pe.wait_ge(o_out, 3 * layer + t + 1)
                    transposes(layer, ("oT", t), [(h * P, P, osb[0:n, h * DK:(h + 1) * DK]) for h in range(HH)])
                for t in range(3):
                    job_read(pe, (layer, "oT", t))
                for j in range(2):
                    project(layer, ("ga", j), range(3), xT, 512, [("ga", j, 0), ("ga", j, 1)])
                    project(layer, ("bra", j), range(3), aT, 512, [("bra", j)])
                    project(layer, ("gb", j), range(3), xT, 512, [("gb", j, 0), ("gb", j, 1)])
                    project(layer, ("brb", j), range(3), oT, 512, [("brb", j)])
                for t in range(3):
                    pe.wait_ge(mg_out, 6 * layer + 4 + t)
                    for h in range(2):
                        transposes(layer, ("mT", t, h), [((c % 4) * P, P, mg[0:NT[t], t, c:D:8]) for c in range(4 * h, 4 * h + 4)])
                for t in range(3):
                    for h in range(2):
                        job_read(pe, (layer, "mT", t, h))
                for j in range(2):
                    project(layer, ("wo", j), range(3), mT, 512, [("wo", j, 0), ("wo", j, 1)])
                for t in range(3):
                    pe.wait_ge(ln_out, 3 * (2 * layer + 1) + t + 1)
                    for h in range(2):
                        transposes(layer, ("t1", t, h), [((c % 4) * P, P, x[0:NT[t], t, c:D:8]) for c in range(4 * h, 4 * h + 4)])
                for t in range(3):
                    for h in range(2):
                        job_read(pe, (layer, "t1", t, h))
                pe.wait_ge(rows_in, 80 * (layer + 1))
                for t in range(3):
                    b = open_bank((layer, "rt", t))
                    for c in range(8):
                        ins = mm(b[0:NT[t], 0:36], xT[:, c, T0[t]:T0[t] + NT[t]], wr[:, c, :], c == 0, c == 7)
                    done(ins)
                pe.wait_ge(ple_in, 48 * (layer + 1))
                for t in range(3):
                    transposes(layer, ("pT", t), [(c * P, P, pin[0:NT[t], t, c:PLE:2]) for c in range(2)])
                for j in range(2):
                    project(layer, ("pg", j), range(3), xT, 512, [("pg", j, 0), ("pg", j, 1)])
                for t in range(3):
                    job_read(pe, (layer, "pT", t))
                n = piece_number(layer, ("pl",))
                arrived(n)
                w = slot(n).rearrange("p (c n) -> p c n", c=2)
                for j in range(2):
                    for t in range(3):
                        b = open_bank((layer, "pl", j, t))
                        for c in range(2):
                            ins = mm(b[0:NT[t], :], pT[:, c, T0[t]:T0[t] + NT[t]], w[:, c, 512 * j:512 * j + 512], c == 0, c == 1)
                        done(ins)
                pe.wait_ge(route_out, 3 * (layer + 1))
                for t in range(3):
                    b = open_bank((layer, "rk", t))
                    for s in range(t):
                        mm(b[0:NT[t], 0:32], ones[:, 0:NT[t]], route[:, s, :], s == 0, False)
                    done(mm(b[0:NT[t], 0:32], tri[0:NT[t], 0:NT[t]], route[0:NT[t], t, :], t == 0, True))
                b = open_bank((layer, "cnt"))
                for t in range(3):
                    ins = mm(b[0:1, 0:32], ones[0:NT[t], 0:1], route[0:NT[t], t, :], t == 0, t == 2)
                done(ins)
                first = layer * LAYER_PIECES + len(PIECES)
                with pe.Fori(0, QUADS) as g:
                    key = lambda *k: (layer, "moe") + k
                    pe.wait_ge(sel_out, (QUADS + 1) * layer + 1 + g)
                    for h in range(2):
                        b = open_bank(key("X", h), g)
                        for c in range(4 * h, 4 * h + 4):
                            for t in range(3):
                                ins = mm(b[:, (c % 4) * P:(c % 4 + 1) * P], x[0:NT[t], t, c:D:8], sel[0:NT[t], t, :], t == 0, t == 2)
                        done(ins)
                    b = open_bank(key("ST"), g)
                    for t in range(3):
                        ins = pe.transpose(b[:, T0[t]:T0[t] + NT[t]], selw[0:NT[t], t, :], ident[0:NT[t], 0:NT[t]])
                    done(ins)
                    job_read(pe, key("X", 0), g)
                    job_read(pe, key("X", 1), g)
                    for m, name in enumerate(("G", "U")):
                        b = open_bank(key(name), g)
                        for h in range(2):
                            ns = [first + 8 * m + 4 * h + e for e in range(QUAD)]
                            for n in ns:
                                arrived(n, g)
                            for c in range(4):
                                for e in range(QUAD):
                                    ins = mm(b[32 * e:32 * e + 32, :], xeT[:, 4 * h + c, 32 * e:32 * e + 32],
                                             slot(ns[e])[:, c * 512:(c + 1) * 512], h + c == 0, h + c == 4)
                            if h == 0:
                                ins.then_inc(halves_used, 1)
                        done(ins)
                    job_read(pe, key("U"), g)
                    b = open_bank(key("hT"), g)
                    for c in range(4):
                        ins = pe.transpose(b[:, c * P:(c + 1) * P], hid[:, c:DE:4], ident)
                    done(ins)
                    job_read(pe, key("hT"), g)
                    ys = [open_bank(key("Y", j), g) for j in range(2)]
                    for h in range(2):
                        ns = [first + 16 + 4 * h + e for e in range(QUAD)]
                        for n in ns:
                            arrived(n, g)
                        for c in range(2):
                            for j in range(2):
                                for e in range(QUAD):
                                    ins = mm(ys[j][32 * e:32 * e + 32, :], hidT[:, 2 * h + c, 32 * e:32 * e + 32],
                                             slot(ns[e])[:, c * D + 512 * j:c * D + 512 * j + 512], h + c == 0, h + c == 2)
                                if h == 1 and c == 1:
                                    done(ins)
                        if h == 0:
                            ins.then_inc(halves_used, 1)
                    for k in (("ST",), ("Y", 0), ("Y", 1)):
                        job_read(pe, key(*k), g)
                    for t in range(3):
                        for j in range(2):
                            b = open_bank(key("C", t, j), g)
                            done(mm(b[0:NT[t], :], selT[:, T0[t]:T0[t] + NT[t]], ye[:, 512 * j:512 * j + 512], True, True))

                def more(g, n):
                    phase = lambda ins: ins.then_inc(more_matmuls, 1)
                    pe.wait_ge(more_chosen, n + 1)
                    for h in range(2):
                        for c in range(4):
                            for t in range(3):
                                mm(banks[h][:, c * P:(c + 1) * P], x[0:NT[t], t, 4 * h + c:D:8], sel[0:NT[t], t, :], t == 0, t == 2)
                    for t in range(3):
                        ins = pe.transpose(banks[2][:, T0[t]:T0[t] + NT[t]], selw[0:NT[t], t, :], ident[0:NT[t], 0:NT[t]])
                    phase(ins)
                    pe.wait_ge(more_read, n * 5 + 1)
                    for m in range(2):
                        for h in range(2):
                            pe.wait_ge(more_weights, n * 384 + 64 * (2 * m + h + 1))
                            for c in range(4):
                                for e in range(QUAD):
                                    ins = mm(banks[3 + m][32 * e:32 * e + 32, :], xeT[:, 4 * h + c, 32 * e:32 * e + 32],
                                             extra_w[e][:, c * 512:(c + 1) * 512], h + c == 0, h + c == 4)
                            phase(ins)
                    pe.wait_ge(more_read, n * 5 + 2)
                    for c in range(4):
                        ins = pe.transpose(banks[5][:, c * P:(c + 1) * P], hid[:, c:DE:4], ident)
                    phase(ins)
                    pe.wait_ge(more_read, n * 5 + 3)
                    for h in range(2):
                        pe.wait_ge(more_weights, n * 384 + 64 * (4 + h + 1))
                        for c in range(2):
                            for j in range(2):
                                for e in range(QUAD):
                                    ins = mm(banks[6 + j][32 * e:32 * e + 32, :], hidT[:, 2 * h + c, 32 * e:32 * e + 32],
                                             extra_w[e][:, c * D + 512 * j:c * D + 512 * j + 512], h + c == 0, h + c == 2)
                        phase(ins)
                    pe.wait_ge(more_read, n * 5 + 4)
                    for t in range(3):
                        for j in range(2):
                            ins = mm(banks[2 * t + j][0:NT[t], :], selT[:, T0[t]:T0[t] + NT[t]], ye[:, 512 * j:512 * j + 512], True, True)
                    phase(ins)
                    pe.wait_ge(more_read, n * 5 + 5)

                for t in range(3):
                    for j in range(2):
                        job_read(pe, (layer, "moe", "C", t, j), QUADS - 1)
                further_passes(pe, layer, turn, more)

        @block.scalar
        def _(act):
            steps = Steps(act, act_step)
            step = steps.step

            def rstd(cols, inp, scale, n, signal):
                step(act.activation(cols, inp, ACT.Ln, bias=eps_col[0:n], scale=scale))
                act.activation(cols, cols, ACT.Exp, scale=-0.5).then_inc(signal, 1)

            def layer_norm(k):
                for t in range(3):
                    act.wait_ge(ln_var, 3 * k + t + 1)
                    n = NT[t]
                    rstd(ln_rs[0:n, t:t + 1], mvs[0:n, 2 * t + 1:2 * t + 2], 1.0, n, ln_rstd)

            def read_x(key_name, layer, dst):
                for t in range(3):
                    key = (layer, key_name, t, 0)
                    job_done(act, key)
                    n = NT[t]
                    src = bank(key)[:, :].rearrange("p (c t) -> p c t", c=4)[:, :, 0:n]
                    emptied(act.copy(dst[:, 0:4, T0[t]:T0[t] + n], src), key)

            turn = act.alloc_register("act_turn")
            act.reg_mov(turn, 0)
            act.wait_ge(eps_set, 1)
            layer_norm(0)
            for layer in range(DEPTH):
                read_x("tx", layer, xT)
                for name, width, cols, junk in (("cq", QL, ssq, 0), ("kv", KVL, ssk, QL)):
                    for t in range(3):
                        key = (layer, name, t)
                        job_done(act, key)
                        n = NT[t]
                        step(act.activation(q[0:n, t, junk:junk + width], bank(key)[0:n, 0:width], ACT.Square,
                                            accum_out=cols[0:n, t:t + 1]))
                        rstd(cols[0:n, t:t + 1], cols[0:n, t:t + 1], 1.0 / width, n, lat_rstd)
                for t in range(3):
                    key = (layer, "f", t)
                    job_done(act, key)
                    n = NT[t]
                    z = bank(key)[0:n, :]
                    act.activation(hk[0:n, t, :], z, ACT.Exp)
                    step(act.activation(lf[0:n, t, :], z, ACT.Abs))
                    step(act.activation(lf[0:n, t, :], lf[0:n, t, :], ACT.Exp, scale=-1.0))
                    act.activation(lf[0:n, t, :], lf[0:n, t, :], ACT.Ln, bias=1.0).then_inc(f_act, 1)
                if layer == 1:
                    act.wait_ge(lb_v, 1)
                    step(act.activation(one_mlb, ln_lb, ACT.Exp))
                    step(act.activation(ln_1mlb, ln_lb, ACT.Abs))
                    step(act.activation(ln_1mlb, ln_1mlb, ACT.Exp, scale=-1.0))
                    act.activation(ln_1mlb, ln_1mlb, ACT.Ln, bias=1.0).then_inc(lb_e, 1)
                    for t in range(3):
                        act.wait_ge(f_gap, t + 1)
                        w = fw[0:NT[t], t, :]
                        step(act.activation(w, w, ACT.Abs))
                        step(act.activation(w, w, ACT.Exp, scale=-1.0))
                        act.activation(w, w, ACT.Ln, bias=1.0).then_inc(f_add, 1)
                for name, dst in (("q", hq), ("i", hv), ("g", hg)):
                    for t in range(3):
                        key = (layer, name, t)
                        job_done(act, key)
                        n = NT[t]
                        if name == "i":
                            emptied(act.copy(dst[0:n, t, :], bank(key)[0:n, :]), key)
                        else:
                            act.activation(dst[0:n, t, :], bank(key)[0:n, :], ACT.Exp, scale=-1.0).then_inc(silu_e, 1)
                for t in range(3):
                    key = (layer, "kvT", t)
                    job_done(act, key)
                    src = bank(key)[:, 0:256].rearrange("p (c t) -> p c t", c=2)[:, :, 0:NT[t]]
                    emptied(act.copy(ckvT[:, :, T0[t]:T0[t] + NT[t]], src), key)
                for h in range(2):
                    for t in range(3):
                        key = (layer, "uq", t, h)
                        job_done(act, key)
                        emptied(act.copy(q[0:NT[t], t, 384 * h:384 * h + 384], bank(key)[0:NT[t], 0:384]), key)
                for t in range(2):
                    key = (layer, "V", t)
                    job_done(act, key)
                    emptied(act.copy(val[:, t, :], bank(key)[:, :]), key)
                for t in range(2):
                    key = (layer, "qT", t, 0)
                    job_done(act, key)
                    src = bank(key)[0:QK, :].rearrange("p (h t) -> p h t", h=4)
                    emptied(act.copy(qT[0:QK, 0:4, T0[t]:T0[t] + P], src), key)
                key = (layer, "qTs")
                job_done(act, key)
                emptied(act.copy(qTs[0:QK, :, :], bank(key)[0:QK, 0:256].rearrange("p (h t) -> p h t", h=HEADS)), key)
                for i in range(2):
                    nkeys = P * (i + 1)
                    per = 512 // nkeys
                    for n in range(HEADS // per):
                        key = (layer, "S", i, n)
                        act.wait_ge(nmax, 8 * layer + 2 * i + n + 1)
                        for k in range(per):
                            h = n * per + k
                            ins = act.activation(prob[:, h, 0:nkeys], bank(key)[:, k * nkeys:(k + 1) * nkeys], ACT.Exp,
                                                 bias=nb[:, h:h + 1], scale=SCALE, accum_out=psum_[:, h:h + 1])
                        emptied(ins, key)
                    for kt in range(i + 1):
                        key = (layer, "PT", i, kt, 0)
                        job_done(act, key)
                        emptied(act.copy(probT[:, kt, 0:4, :], bank(key)[:, :].rearrange("p (h t) -> p h t", h=4)), key)
                    key = (layer, "aT", i)
                    job_done(act, key)
                    emptied(act.copy(aT[:, :, T0[i]:T0[i] + P], bank(key)[:, :].rearrange("p (c t) -> p c t", c=4)), key)
                for k in range(4):
                    key = (layer, "cc", k)
                    job_done(act, key)
                    b = bank(key)
                    act.copy(cT[:, :, k * P:(k + 1) * P], b[:, 0:256].rearrange("p (c t) -> p c t", c=2))
                    emptied(act.copy(kcT[0:QK, k * P:(k + 1) * P], b[0:QK, 256:384]), key)
                key = (layer, "ql")
                job_done(act, key)
                emptied(act.copy(qlatT[:, :, :], bank(key)[:, :].rearrange("p (c t) -> p c t", c=2)), key)
                new = bank((layer, "ss", 2))
                for r in range(2):
                    key = (layer, "ss", r)
                    act.wait_ge(nmax, 8 * layer + 8)
                    act.activation(prob_s[:, r, 0:PAST], bank(key)[:, :], ACT.Exp, bias=nb[:, r:r + 1],
                                   scale=SCALE, accum_out=psum_[:, 2 * r:2 * r + 1]).then_inc(bank_emptied[book.bank(key)], 1)
                    ins = act.activation(prob_s[:, r, PAST:KEYS], new[:, r * DEC:(r + 1) * DEC], ACT.Exp,
                                         bias=nb[:, r:r + 1], scale=SCALE, accum_out=psum_[:, 2 * r + 1:2 * r + 2])
                    if r == 0:
                        ins.then_inc(smax_s, 1)
                    else:
                        emptied(ins, (layer, "ss", 2))
                for i in (0, 2):
                    key = (layer, "PTs", i)
                    job_done(act, key)
                    if i == 0:
                        ins = act.copy(probT_s[:, 0:2, :], bank(key)[:, :].rearrange("p (k t) -> p k t", k=2))
                    else:
                        ins = act.copy(probT_s[0:DEC, 4, :], bank(key)[0:DEC, 0:256])
                    emptied(ins, key)
                key = (layer, "lat")
                job_done(act, key)
                emptied(act.copy(latT[:, :, :], bank(key)[:, :].rearrange("p (c t) -> p c t", c=2)), key)
                key = (layer, "aTs")
                job_done(act, key)
                emptied(act.copy(aT[:, :, T0[2]:T], bank(key)[:, 0:128].rearrange("p (c t) -> p c t", c=4)), key)
                for t in range(3):
                    n = NT[t]
                    nbk = 2 if t < 2 else 1
                    wcols = 512 if t < 2 else 6 * n
                    key = (layer, "hq", t)
                    job_done(act, key)
                    emptied(act.copy(hqT[:, :, 0:n], bank(key)[:, :].rearrange("p (h t) -> p h t", h=HH)[:, :, 0:n]), key)
                    key = (layer, "suf", t)
                    job_done(act, key)
                    emptied(act.activation(osb[0:n, :], bank(key)[0:n, :], ACT.Exp), key)
                    for h in range(HH):
                        at = (3 * layer + t) * HH + h
                        if at >= 2:
                            act.wait_ge(qh_out, at - 1)
                            act.wait_ge(kh_out, at - 1)
                        for k in range(nbk):
                            key = (layer, "E", t, h, k)
                            job_done(act, key)
                            emptied(act.activation(dec[h % 2][:, 512 * k:512 * k + wcols], bank(key)[:, 0:wcols], ACT.Exp), key)
                    key = (layer, "o", t)
                    job_done(act, key)
                    for h in range(HH):
                        c = slice(h * DK, (h + 1) * DK)
                        ins = act.activation(hq[0:n, t, c], bank(key)[0:n, c], ACT.Square,
                                             accum_out=oss[0:n, 4 * t + h:4 * t + h + 1])
                    step(ins)
                    o4 = oss[0:n, 4 * t:4 * t + 4]
                    rstd(o4, o4, 1.0 / DK, n, o_sq)
                    key = (layer, "oT", t)
                    job_done(act, key)
                    emptied(act.copy(oT[:, :, T0[t]:T0[t] + n], bank(key)[:, :].rearrange("p (h t) -> p h t", h=HH)[:, :, 0:n]), key)
                for j in range(2):
                    for name, dst in (("ga", gate_a), ("gb", gate_b)):
                        for t in range(3):
                            n = NT[t]
                            key = (layer, name, j, t)
                            if j == 1 and name == "ga":
                                job_read(act, (layer, "bra", 0, t))
                            if j == 1 and name == "gb":
                                act.wait_ge(mg_out, 6 * layer + t + 1)
                            job_done(act, key)
                            emptied(act.activation(dst[0:n, t, :], bank(key)[0:n, :], ACT.Exp, scale=-1.0), key)
                read_x("mT", layer, mT)
                layer_norm(1 + 2 * layer)
                read_x("t1", layer, xT)
                for t in range(3):
                    key = (layer, "pT", t)
                    job_done(act, key)
                    src = bank(key)[:, 0:256].rearrange("p (c t) -> p c t", c=2)[:, :, 0:NT[t]]
                    emptied(act.copy(pT[:, :, T0[t]:T0[t] + NT[t]], src), key)
                for t in range(3):
                    n = NT[t]
                    act.wait_ge(route_e, 3 * layer + t + 1)
                    r = rsm[0:n, t, :]
                    act.activation(r[:, 18:22], rl[0:n, t, 0:4], ACT.Exp, bias=r[:, 17:18], accum_out=r[:, 22:23])
                    act.activation(r[:, 43:44], r[:, 25:26], ACT.Exp, bias=r[:, 42:43]).then_inc(route_v, 1)
                for j in range(2):
                    for t in range(3):
                        n = NT[t]
                        key = (layer, "pg", j, t)
                        job_done(act, key)
                        emptied(act.activation(pgate[0:n, t, 512 * j:512 * j + 512], bank(key)[0:n, :], ACT.Exp, scale=-1.0), key)
                with act.Fori(0, QUADS) as g:
                    key = (layer, "moe", "X", 0)
                    job_done(act, key, g)
                    emptied(act.copy(xeT[:, 0:4, :], bank(key)[:, :].rearrange("p (c t) -> p c t", c=4)), key)
                    key = (layer, "moe", "ST")
                    job_done(act, key, g)
                    emptied(act.copy(selT[:, 0:T], bank(key)[:, 0:T]), key)
                    key = (layer, "moe", "G")
                    job_done(act, key, g)
                    act.activation(eh[:, :], bank(key)[:, :], ACT.Exp, scale=-1.0).then_inc(eh_out, 1)
                    key = (layer, "moe", "hT")
                    job_done(act, key, g)
                    emptied(act.copy(hidT[:, :, :], bank(key)[:, :].rearrange("p (c t) -> p c t", c=4)), key)
                    key = (layer, "moe", "Y", 0)
                    job_done(act, key, g)
                    emptied(act.copy(ye[:, 0:512], bank(key)[:, :]), key)

                experts = [w[layer].rearrange("e (p h c) n -> e p h (c n)", p=P, h=2) for w in (w_e_gate, w_e_up, w_e_down)]

                def more(g, n):
                    for r in range(6):
                        act.wait_ge(more_matmuls, n * 9 + 1 + (0, 2, 3, 4, 5, 7)[r])
                        for e in range(QUAD):
                            src = experts[r // 2][bass.ds(g * QUAD + e, 1), :, r % 2, :].rearrange("e p n -> p (e n)")
                            act.dma_start(extra_w[e], src).then_inc(more_weights, 16)
                        if r == 2:
                            act.activation(eh[:, :], banks[3][:, :], ACT.Exp, scale=-1.0).then_inc(more_exp, 1)

                further_passes(act, layer, turn, more)
                layer_norm(2 + 2 * layer)

        @block.vector
        def _(dve):
            steps = Steps(dve, vec_step)
            step = steps.step

            def layer_norm(k, src):
                for t in range(3):
                    n = NT[t]
                    dve.bn_stats(ln_st[0:n, 0:6], src[0:n, t, 0:512])
                    step(dve.bn_stats(ln_st[0:n, 6:12], src[0:n, t, 512:1024]))
                    dve.bn_aggr(mvs[0:n, 2 * t:2 * t + 2], ln_st[0:n, :]).then_inc(ln_var, 1)
                    dve.wait_ge(ln_var, 3 * k + t + 1)
                dve.wait_ge(lnw_in, 32 * (k + 1))
                for t in range(3):
                    n = NT[t]
                    dve.wait_ge(ln_rstd, 3 * k + t + 1)
                    xt = x[0:n, t, :]
                    step(dve.tensor_scalar(xt, src[0:n, t, :], mvs[0:n, 2 * t:2 * t + 1], ln_rs[0:n, t:t + 1], ALU.subtract, ALU.mult))
                    step(dve.tensor_tensor(xt, xt, lnw[0:n, 0, :], ALU.mult))
                    dve.tensor_tensor(xt, xt, lnw[0:n, 1, :], ALU.add).then_inc(ln_out, 1)

            def read_x(key_name, layer, dst):
                for t in range(3):
                    key = (layer, key_name, t, 1)
                    job_done(dve, key)
                    n = NT[t]
                    src = bank(key)[:, :].rearrange("p (c t) -> p c t", c=4)[:, :, 0:n]
                    emptied(dve.tensor_copy(dst[:, 4:8, T0[t]:T0[t] + n], src), key)

            def rope(dst, src, n, t, heads):
                tab = cst[0:n, C_ROPE + 64 * t:C_ROPE + 64 * (t + 1)]
                cs, sn = bcast(tab[:, 0:32], 1, heads), tab[:, 32:64]
                turned = rtmp[0:n, 0:heads, 0:32]
                dve.tensor_tensor(turned[:, :, 0:16], src[:, :, 16:32], bcast(sn[:, 0:16], 1, heads), ALU.mult)
                step(dve.tensor_tensor(turned[:, :, 16:32], src[:, :, 0:16], bcast(sn[:, 16:32], 1, heads), ALU.mult))
                step(dve.tensor_tensor(rtmp[0:n, 0:heads, 32:64], src, cs, ALU.mult))
                return dve.tensor_tensor(dst, turned, rtmp[0:n, 0:heads, 32:64], ALU.add)

            def one_over_1p(a):
                step(dve.tensor_scalar(a, a, 1.0, None, ALU.add))
                step(dve.reciprocal(a, a))

            turn = dve.alloc_register("dve_turn")
            dve.reg_mov(turn, 0)
            dve.wait_ge(x_in, 48)
            layer_norm(0, x)
            dve.wait_ge(consts_in, 16)
            for layer in range(DEPTH):
                read_x("tx", layer, xT)
                dve.wait_ge(rows_in, 80 * (layer + 1))
                dve.wait_ge(zeroed, 3 * layer + 3)
                for t in range(3):
                    key = (layer, "cq", t)
                    n = NT[t]
                    dve.wait_ge(lat_rstd, 6 * layer + t + 1)
                    emptied(dve.scalar_tensor_tensor(cq[0:n, t, :], bank(key)[0:n, 0:QL], ssq[0:n, t:t + 1],
                                                     qn_row[0:n, :], ALU.mult, ALU.mult), key)
                for t in range(3):
                    key = (layer, "kv", t)
                    n = NT[t]
                    dve.wait_ge(lat_rstd, 6 * layer + 3 + t + 1)
                    b = bank(key)
                    rope(krp[0:n, t:t + 1, NOPE:QK], b[0:n, KVL:KVL + 32].unsqueeze(1), n, t, 1).then_inc(kr_out, 1)
                    dve.wait_ge(kr_out, 3 * layer + t + 1)
                    emptied(dve.scalar_tensor_tensor(ckv[0:n, t, :], b[0:n, 0:KVL], ssk[0:n, t:t + 1],
                                                     kn_row[0:n, :], ALU.mult, ALU.mult), key)
                if layer == 1:
                    dve.wait_ge(lb_in, 32)
                    dve.tensor_tensor(ln_lb, fw[:, 1, :], fw[:, 0, :], ALU.subtract).then_inc(lb_v, 1)
                    dve.wait_ge(lb_e, 1)
                    one_over_1p(one_mlb)
                    step(dve.tensor_scalar(lbtmp, ln_lb, -1.0, 0.0, ALU.mult, ALU.min))
                    step(dve.scalar_tensor_tensor(ln_lb, ln_lb, 0.0, ln_1mlb, ALU.min, ALU.subtract))
                    step(dve.tensor_tensor(ln_1mlb, lbtmp, ln_1mlb, ALU.subtract))
                for t in range(3):
                    key = (layer, "f", t)
                    n = NT[t]
                    dve.wait_ge(f_act, 3 * layer + t + 1)
                    ft, kt = lf[0:n, t, :], hk[0:n, t, :]
                    ins = dve.scalar_tensor_tensor(ft, bank(key)[0:n, :], 0.0, ft, ALU.min, ALU.subtract)
                    emptied(ins, key)
                    if layer == 0:
                        step(dve.tensor_scalar(kt, kt, 1.0, None, ALU.add))
                        dve.reciprocal(kt, kt).then_inc(hk_out, 1)
                        job_read(dve, key)
                    else:
                        one_over_1p(kt)
                        dve.tensor_tensor(kt, kt, one_mlb[0:n, :], ALU.mult).then_inc(hk_out, 1)
                        job_read(dve, key)
                        step(dve.tensor_tensor(ft, ft, ln_1mlb[0:n, :], ALU.add))
                        dve.tensor_tensor(fw[0:n, t, :], ft, ln_lb[0:n, :], ALU.subtract).then_inc(f_gap, 1)
                        step(dve.tensor_tensor(ft, ft, ln_lb[0:n, :], ALU.max))
                for name, dst, base in (("q", hq, 0), ("g", hg, 3)):
                    if name == "g" and layer == 1:
                        for t in range(3):
                            n = NT[t]
                            dve.wait_ge(f_add, t + 1)
                            dve.tensor_tensor(lf[0:n, t, :], lf[0:n, t, :], fw[0:n, t, :], ALU.add).then_inc(lf_out, 1)
                    for t in range(3):
                        key = (layer, name, t)
                        n = NT[t]
                        dve.wait_ge(silu_e, 6 * layer + base + t + 1)
                        one_over_1p(dst[0:n, t, :])
                        emptied(dve.tensor_tensor(dst[0:n, t, :], dst[0:n, t, :], bank(key)[0:n, :], ALU.mult), key)
                if layer == 0:
                    dve.sem_inc(lf_out, 3)
                for t in range(3):
                    key = (layer, "cT", t)
                    n = NT[t]
                    job_done(dve, key)
                    b = bank(key)
                    dve.tensor_copy(cqT[:, :, T0[t]:T0[t] + n], b[:, 0:384].rearrange("p (c t) -> p c t", c=3)[:, :, 0:n])
                    if t < 2:
                        ins = dve.tensor_copy(kT[NOPE:QK, :, T0[t]:T0[t] + P], bcast(b[NOPE:QK, 384:512], 1, HEADS))
                    else:
                        ins = dve.tensor_copy(kcT[0:QK, PAST:KEYS], b[0:QK, 384:384 + n])
                    emptied(ins, key)
                for i in range(4):
                    key = (layer, "kT", i)
                    job_done(dve, key)
                    emptied(dve.tensor_copy(kT[0:NOPE, 2 * i:2 * i + 2, :], bank(key)[0:NOPE, :].rearrange("p (h t) -> p h t", h=2)), key)
                for t in range(3):
                    n = NT[t]
                    job_read(dve, (layer, "uq", t, 0))
                    job_read(dve, (layer, "uq", t, 1))
                    qr = q[0:n, t, :].rearrange("p (h c) -> p h c", h=HEADS)[:, :, NOPE:QK]
                    rope(qr, qr, n, t, HEADS).then_inc(q_out, 1)
                    dve.wait_ge(q_out, 3 * layer + t + 1)
                for t in range(2):
                    key = (layer, "qT", t, 1)
                    job_done(dve, key)
                    emptied(dve.tensor_copy(qT[0:QK, 4:8, T0[t]:T0[t] + P], bank(key)[0:QK, :].rearrange("p (h t) -> p h t", h=4)), key)
                for i in range(2):
                    nkeys = P * (i + 1)
                    per = 512 // nkeys
                    for n in range(HEADS // per):
                        key = (layer, "S", i, n)
                        hs = slice(n * per, (n + 1) * per)
                        job_done(dve, key)
                        step(dve.reduce_max(mx[:, hs], bank(key)[:, :].rearrange("p (h k) -> p h k", h=per), AX.X))
                        dve.tensor_scalar(nb[:, hs], mx[:, hs], -SCALE, None, ALU.mult).then_inc(nmax, 1)
                    for n in range(HEADS // per):
                        hs = slice(n * per, (n + 1) * per)
                        job_read(dve, (layer, "S", i, n))
                        step(dve.reciprocal(prec[:, hs], psum_[:, hs]))
                        pr = prob[:, hs, 0:nkeys]
                        dve.tensor_tensor(pr, pr, bcast(prec[:, hs], 2, nkeys), ALU.mult).then_inc(prob_out, 1)
                    for kt in range(i + 1):
                        key = (layer, "PT", i, kt, 1)
                        job_done(dve, key)
                        emptied(dve.tensor_copy(probT[:, kt, 4:8, :], bank(key)[:, :].rearrange("p (h t) -> p h t", h=4)), key)
                for i in range(4):
                    key = (layer, "wuT", i)
                    job_done(dve, key)
                    emptied(dve.tensor_copy(wukT[0:NOPE, 2 * i:2 * i + 2, :, :].rearrange("p h c k -> p (h c k)"), bank(key)[0:NOPE, :]), key)
                new = bank((layer, "ss", 2))
                job_done(dve, (layer, "ss", 2))
                for r in range(2):
                    key = (layer, "ss", r)
                    dve.reduce_max(mx[:, 2 * r:2 * r + 1], bank(key)[:, :], AX.X)
                    step(dve.reduce_max(mx[:, 2 * r + 1:2 * r + 2], new[:, r * DEC:(r + 1) * DEC], AX.X))
                    step(dve.tensor_tensor(mx[:, 2 * r:2 * r + 1], mx[:, 2 * r:2 * r + 1], mx[:, 2 * r + 1:2 * r + 2], ALU.max))
                    dve.tensor_scalar(nb[:, r:r + 1], mx[:, 2 * r:2 * r + 1], -SCALE, None, ALU.mult).then_inc(nmax, 1)
                for r in range(2):
                    if r == 0:
                        dve.wait_ge(smax_s, layer + 1)
                    else:
                        job_read(dve, (layer, "ss", 2))
                    s0 = psum_[:, 2 * r:2 * r + 1]
                    step(dve.tensor_tensor(prec[:, r:r + 1], s0, psum_[:, 2 * r + 1:2 * r + 2], ALU.add))
                    step(dve.reciprocal(prec[:, r:r + 1], prec[:, r:r + 1]))
                    pr = prob_s[:, r, :]
                    dve.tensor_scalar(pr, pr, prec[:, r:r + 1], None, ALU.mult).then_inc(prob_s_out, 1)
                key = (layer, "PTs", 1)
                job_done(dve, key)
                emptied(dve.tensor_copy(probT_s[:, 2:4, :], bank(key)[:, :].rearrange("p (k t) -> p k t", k=2)), key)
                for t in range(3):
                    n = NT[t]
                    nbk = 2 if t < 2 else 1
                    lo = 0 if t < 2 else 2
                    nl = 7 - lo
                    key = (layer, "hk", t)
                    job_done(dve, key)
                    emptied(dve.tensor_copy(hkT[:, :, 0:n], bank(key)[:, :].rearrange("p (h t) -> p h t", h=HH)[:, :, 0:n]), key)
                    job_read(dve, key)
                    job_read(dve, (layer, "hq", t))
                    job_read(dve, (layer, "suf", t))
                    dve.tensor_tensor(hk[0:n, t, :], hk[0:n, t, :], osb[0:n, :], ALU.mult).then_inc(ksuf_out, 1)

                    def products(h):
                        for k in range(nbk):
                            job_read(dve, (layer, "E", t, h, k))
                        if h >= 2:
                            job_done(dve, (layer, "A", t, h - 2, nbk - 1))
                        d = dec[h % 2][:, 0:(nl + 1) * n].rearrange("p (l t) -> p l t", l=nl + 1)
                        qo = qh[h % 2][:, 0:nl * n].rearrange("p (l t) -> p l t", l=nl)
                        ko = kh[h % 2][:, 0:nl * n].rearrange("p (l t) -> p l t", l=nl)
                        dve.tensor_copy(bend[:, 4 * t + h:4 * t + h + 1], d[:, nl, n - 1:n])
                        dve.tensor_tensor(qcum[:, h, 0:n], d[:, nl, :], hqT[:, h, 0:n], ALU.mult)
                        dve.tensor_tensor(qo, d[:, 0:nl, :], bcast(hqT[:, h, 0:n], 1, nl), ALU.mult).then_inc(qh_out, 1)
                        dve.tensor_tensor(ko, d[:, 0:nl, :], bcast(hkT[:, h, 0:n], 1, nl), ALU.mult).then_inc(kh_out, 1)

                    products(0)
                    for h in range(HH):
                        if h < HH - 1:
                            products(h + 1)
                        at = (3 * layer + t) * HH + h + 1
                        a = am[h % 2][:, 0:(nl + 1) * n].rearrange("p (l t) -> p l t", l=nl + 1)
                        for k in range(nbk):
                            key = (layer, "A", t, h, k)
                            job_done(dve, key)
                            ls = slice(4 * k, 4 * k + 4) if nbk == 2 else slice(0, nl + 1)
                            m = maskc[0:n, lo:8, 0:n][:, ls, :]
                            nn = m.shape[1]
                            src = bank(key)[0:n, 0:nn * n].rearrange("p (l t) -> p l t", l=nn)
                            emptied(dve.tensor_tensor(a[0:n, ls, :], src, m, ALU.mult), key)
                        for k in range(nbk):
                            job_read(dve, (layer, "A", t, h, k))
                        dve.reduce_sum(att[0:n, h, 0:n], a[0:n, :, :].rearrange("p l t -> p t l"), AX.X).then_inc(att_out, 1)
                    key = (layer, "o", t)
                    dve.wait_ge(o_sq, 3 * layer + t + 1)
                    for h in range(HH):
                        c = slice(h * DK, (h + 1) * DK)
                        ins = dve.scalar_tensor_tensor(osb[0:n, c], bank(key)[0:n, c], oss[0:n, 4 * t + h:4 * t + h + 1],
                                                       hn_row[0:n, c], ALU.mult, ALU.mult)
                    emptied(ins, key)
                    job_read(dve, key)
                    job_read(dve, (layer, "g", t))
                    dve.tensor_tensor(osb[0:n, :], osb[0:n, :], hg[0:n, t, :], ALU.mult).then_inc(o_out, 1)
                    key = (layer, "Sn", t)
                    job_done(dve, key)
                    if t == 0:
                        dve.wait_ge(zeroed, 3 * layer + 4)
                    if t == 2:
                        dve.wait_ge(state_in, 16 * (layer + 1))
                    st = state[0 if t < 2 else 1]
                    for h in range(HH):
                        c = slice(h * DK, (h + 1) * DK)
                        ins = dve.scalar_tensor_tensor(st[:, h, :], st[:, h, :], bend[:, 4 * t + h:4 * t + h + 1],
                                                       bank(key)[:, c], ALU.mult, ALU.add)
                    emptied(ins, key)
                    job_read(dve, key)
                for j in range(2):
                    cols = slice(512 * j, 512 * j + 512)
                    for t in range(3):
                        n = NT[t]
                        job_read(dve, (layer, "ga", j, t))
                        one_over_1p(gate_a[0:n, t, :])
                    for t in range(3):
                        n = NT[t]
                        key = (layer, "bra", j, t)
                        job_done(dve, key)
                        emptied(dve.tensor_tensor(mg[0:n, t, cols], gate_a[0:n, t, :], bank(key)[0:n, :], ALU.mult), key)
                    for t in range(3):
                        n = NT[t]
                        job_read(dve, (layer, "gb", j, t))
                        one_over_1p(gate_b[0:n, t, :])
                    for t in range(3):
                        n = NT[t]
                        key = (layer, "brb", j, t)
                        job_done(dve, key)
                        emptied(dve.tensor_tensor(gate_b[0:n, t, :], gate_b[0:n, t, :], bank(key)[0:n, :], ALU.mult), key)
                        job_read(dve, key)
                        dve.tensor_tensor(mg[0:n, t, cols], mg[0:n, t, cols], gate_b[0:n, t, :], ALU.add).then_inc(mg_out, 1)
                read_x("mT", layer, mT)
                for j in range(2):
                    cols = slice(512 * j, 512 * j + 512)
                    for t in range(3):
                        n = NT[t]
                        key = (layer, "wo", j, t)
                        job_done(dve, key)
                        emptied(dve.scalar_tensor_tensor(x[0:n, t, cols], x[0:n, t, cols], ALPHA, bank(key)[0:n, :],
                                                         ALU.mult, ALU.add), key)
                        job_read(dve, key)
                layer_norm(1 + 2 * layer, x)
                read_x("t1", layer, xT)
                for t in range(3):
                    n = NT[t]
                    key = (layer, "rt", t)
                    r = rsm[0:n, t, :]
                    ri = r.bitcast(U32)
                    lg = rl[0:n, t, :]
                    job_done(dve, key)
                    dve.memset(lg[:, 4:8], -BIG)
                    dve.tensor_copy(lg[:, 0:4], bank(key)[0:n, 0:4])
                    emptied(dve.tensor_copy(lg[:, 8:40], bank(key)[0:n, 4:36]), key)
                    job_read(dve, key)
                    step(dve.max(r[:, 0:8], lg[:, 0:8]))
                    step(dve.max_index(ri[:, 8:16], r[:, 0:8], lg[:, 0:8]))
                    step(dve.tensor_copy(r[:, 16:17], ri[:, 8:9]))
                    dve.tensor_scalar(r[:, 17:18], r[:, 0:1], -1.0, None, ALU.mult)
                    step(dve.tensor_scalar(r[:, 48:52], iota[0:n, 0:4], r[:, 16:17], None, ALU.is_equal))
                    step(dve.tensor_scalar(r[:, 52:56], r[:, 48:52], BIG, -BIG, ALU.mult, ALU.add))
                    e4 = lg[:, 8:40].rearrange("p (g e) -> p g e", g=GROUPS)
                    step(dve.tensor_tensor(e4, e4, bcast(r[:, 48:52], 2, PER_GROUP), ALU.mult))
                    step(dve.tensor_tensor(e4, e4, bcast(r[:, 52:56], 2, PER_GROUP), ALU.add))
                    step(dve.max(r[:, 24:32], lg[:, 8:40]))
                    step(dve.max_index(ri[:, 32:40], r[:, 24:32], lg[:, 8:40]))
                    step(dve.tensor_copy(r[:, 40:42], ri[:, 32:34]))
                    dve.tensor_scalar(r[:, 42:43], r[:, 24:25], -1.0, None, ALU.mult).then_inc(route_e, 1)
                    oh = onehot[0:n, t, :]
                    dve.tensor_scalar(oh[:, 0:32], iota[0:n, :], r[:, 40:41], None, ALU.is_equal)
                    step(dve.tensor_scalar(oh[:, 32:64], iota[0:n, :], r[:, 41:42], None, ALU.is_equal))
                    dve.tensor_tensor(route[0:n, t, :], oh[:, 0:32], oh[:, 32:64], ALU.add).then_inc(route_out, 1)
                for t in range(3):
                    n = NT[t]
                    r = rsm[0:n, t, :]
                    oh = onehot[0:n, t, :]
                    dve.wait_ge(route_v, 3 * layer + t + 1)
                    step(dve.tensor_scalar(r[:, 44:45], r[:, 43:44], 1.0, None, ALU.add))
                    step(dve.tensor_tensor(r[:, 44:45], r[:, 44:45], r[:, 22:23], ALU.mult))
                    step(dve.reciprocal(r[:, 44:45], r[:, 44:45]))
                    step(dve.tensor_tensor(r[:, 45:46], r[:, 44:45], r[:, 43:44], ALU.mult))
                    step(dve.memset(wsel[0:n, t, :], 0.0))
                    step(dve.tensor_scalar(wsel[0:n, t, 0:32], oh[:, 0:32], r[:, 44:45], None, ALU.mult))
                    step(dve.scalar_tensor_tensor(wsel[0:n, t, 0:32], oh[:, 32:64], r[:, 45:46], wsel[0:n, t, 0:32], ALU.mult, ALU.add))
                for j in range(2):
                    cols = slice(512 * j, 512 * j + 512)
                    for t in range(3):
                        job_read(dve, (layer, "pg", j, t))
                        one_over_1p(pgate[0:NT[t], t, cols])
                for j in range(2):
                    cols = slice(512 * j, 512 * j + 512)
                    for t in range(3):
                        n = NT[t]
                        key = (layer, "pl", j, t)
                        job_done(dve, key)
                        emptied(dve.tensor_tensor(pgate[0:n, t, cols], pgate[0:n, t, cols], bank(key)[0:n, :], ALU.mult), key)
                        job_read(dve, key)
                        step(dve.scalar_tensor_tensor(acc[0:n, t, cols], x[0:n, t, cols], ALPHA, pgate[0:n, t, cols], ALU.mult, ALU.add))
                for t in range(3):
                    n = NT[t]
                    key = (layer, "rk", t)
                    job_done(dve, key)
                    step(dve.memset(posm[0:n, t, :], 0.0))
                    emptied(dve.scalar_tensor_tensor(posm[0:n, t, 0:32], bank(key)[0:n, 0:32], 1.0, route[0:n, t, :], ALU.add, ALU.mult), key)
                    job_read(dve, key)
                    step(dve.tensor_scalar(posm[0:n, t, :], posm[0:n, t, :], -1.0, None, ALU.add))
                key = (layer, "cnt")
                job_done(dve, key)
                step(dve.reduce_max(rsm[0:1, 0, 1:9], bank(key)[0:1, 0:32].rearrange("p (q e) -> p q e", e=QUAD), AX.X))
                emptied(dve.reduce_max(rsm[0:1, 0, 0:1], bank(key)[0:1, 0:32], AX.X), key)
                job_read(dve, key)
                dve.tensor_copy(counts[0:1, 0:9], rsm[0:1, 0, 0:9]).then_inc(counts_out, 1)

                def choose(first, step=step):
                    for t in range(3):
                        n = NT[t]
                        s4 = sel[0:n, t, :].rearrange("p (e s) -> p e s", e=QUAD)
                        w4 = selw[0:n, t, :].rearrange("p (e s) -> p e s", e=QUAD)
                        step(dve.tensor_tensor(s4, bcast(iota[0:n, :], 1, QUAD), bcast(posm[0:n, t, first], 2, CAP), ALU.is_equal))
                        ins = dve.tensor_tensor(w4, s4, bcast(wsel[0:n, t, first], 2, CAP), ALU.mult)
                    return ins

                choose(slice(0, QUAD)).then_inc(sel_out, 1)
                steps.enter(5)
                with dve.Fori(0, QUADS) as g:
                    steps.g = g
                    key = (layer, "moe", "X", 1)
                    job_done(dve, key, g)
                    emptied(dve.tensor_copy(xeT[:, 4:8, :], bank(key)[:, :].rearrange("p (c t) -> p c t", c=4)), key)
                    dve.wait_ge(eh_out, QUADS * layer + 1 + g)
                    one_over_1p(eh[:, :])
                    key = (layer, "moe", "G")
                    emptied(dve.tensor_tensor(eh[:, :], eh[:, :], bank(key)[:, :], ALU.mult), key)
                    job_read(dve, key, g)
                    key = (layer, "moe", "U")
                    job_done(dve, key, g)
                    emptied(dve.tensor_tensor(hid[:, :], eh[:, :], bank(key)[:, :], ALU.mult), key)
                    key = (layer, "moe", "Y", 1)
                    job_done(dve, key, g)
                    emptied(dve.tensor_copy(ye[:, 512:1024], bank(key)[:, :]), key)
                    choose(bass.ds(g * QUAD + QUAD, QUAD)).then_inc(sel_out, 1)
                    for t in range(3):
                        for j in range(2):
                            n = NT[t]
                            key = (layer, "moe", "C", t, j)
                            a = acc[0:n, t, 512 * j:512 * j + 512]
                            job_done(dve, key, g)
                            emptied(dve.tensor_tensor(a, a, bank(key)[0:n, :], ALU.add), key)
                steps.leave(QUADS)
                for t in range(3):
                    for j in range(2):
                        job_read(dve, (layer, "moe", "C", t, j), QUADS - 1)

                def next_pass():
                    for t in range(3):
                        ins = dve.tensor_scalar(posm[0:NT[t], t, :], posm[0:NT[t], t, :], float(-CAP), None, ALU.add)
                    dve.drain()

                def more(g, n):
                    settle = lambda ins: dve.drain()
                    choose(bass.ds(g * QUAD, QUAD), settle).then_inc(more_chosen, 1)
                    dve.wait_ge(more_matmuls, n * 9 + 2)
                    for h in range(2):
                        dve.tensor_copy(xeT[:, 4 * h:4 * h + 4, :], banks[h][:, :].rearrange("p (c t) -> p c t", c=4))
                    dve.tensor_copy(selT[:, 0:T], banks[2][:, 0:T]).then_inc(more_read, 1)
                    dve.wait_ge(more_exp, n + 1)
                    settle(dve.tensor_scalar(eh[:, :], eh[:, :], 1.0, None, ALU.add))
                    settle(dve.reciprocal(eh[:, :], eh[:, :]))
                    settle(dve.tensor_tensor(eh[:, :], eh[:, :], banks[3][:, :], ALU.mult))
                    dve.wait_ge(more_matmuls, n * 9 + 6)
                    dve.tensor_tensor(hid[:, :], eh[:, :], banks[4][:, :], ALU.mult).then_inc(more_read, 1)
                    dve.wait_ge(more_matmuls, n * 9 + 7)
                    dve.tensor_copy(hidT[:, :, :], banks[5][:, :].rearrange("p (c t) -> p c t", c=4)).then_inc(more_read, 1)
                    dve.wait_ge(more_matmuls, n * 9 + 9)
                    dve.tensor_copy(ye[:, 0:512], banks[6][:, :])
                    dve.tensor_copy(ye[:, 512:D], banks[7][:, :]).then_inc(more_read, 1)
                    dve.wait_ge(more_matmuls, n * 9 + 10)
                    for t in range(3):
                        for j in range(2):
                            a = acc[0:NT[t], t, 512 * j:512 * j + 512]
                            ins = dve.tensor_tensor(a, a, banks[2 * t + j][0:NT[t], :], ALU.add)
                    ins.then_inc(more_read, 1)
                    dve.wait_ge(more_read, n * 5 + 5)

                further_passes(dve, layer, turn, more, next_pass)
                layer_norm(2 + 2 * layer, acc)


_NAMES = ['x_prompt', 'x_sample', 'p_prompt', 'p_sample', 'cache_ckv', 'cache_krope', 'state_hgrn', 'ln0_g', 'ln0_b',
          'w_in', 'q_norm', 'w_uq', 'kv_norm', 'w_uk', 'w_uv', 'hg_lb', 'hg_norm', 'w_br_a', 'w_br_b', 'w_out',
          'ln1_g', 'ln1_b', 'w_router_group', 'w_router_expert', 'w_e_gate', 'w_e_up', 'w_e_down', 'w_ple',
          'w_ple_gate', 'ln2_g', 'ln2_b']
_OUTS = [(1, SEQ, D), (1, DEC, D), (DEPTH, 1, SEQ, KVL), (DEPTH, 1, SEQ, ROPE), (DEPTH, 1, HH, DK, DK),
         (DEPTH, 1, DEC, KVL), (DEPTH, 1, DEC, ROPE), (DEPTH, 1, HH, DK, DK)]


def kernel(**inputs):
    import concourse.bacc as bacc
    from concourse.bass_utils import run_bass_kernel_spmd

    nc = bacc.Bacc("TRN2", target_bir_lowering=False, num_devices=1)
    arrays = {f"in_{n}": np.ascontiguousarray(inputs[n]) for n in _NAMES}
    arrays["in_consts"] = constants()
    arrays["in_masks"] = mask_rows()
    args = [nc.dram_tensor(n, a.shape, mybir.dt.from_np(a.dtype), kind="ExternalInput").ap() for n, a in arrays.items()]
    args += [nc.dram_tensor(f"out_{i}", s, F32, kind="ExternalOutput").ap() for i, s in enumerate(_OUTS)]
    build(nc, *args)
    r = run_bass_kernel_spmd(nc, [arrays], core_ids=[0])
    return tuple(r.results[0][f"out_{i}"] for i in range(len(_OUTS)))
```
